# Optimizing a Trainium2 kernel written in Bass

```python
import math
import jax, jax.numpy as jnp
from jax import lax
import numpy as np

D_MODEL = 1024
BATCH = 1
SEQ = 512
DEPTH = 2
DEC_BATCH = 8
DEC_SEQ = 4
PAST_LEN = 4096
PAGE_SIZE = 128

HEAD_DIM = 64
N_HEADS = D_MODEL // HEAD_DIM
N_KV_HEADS_A = 4
WINDOW_A = 128
DILATED_GROUPS = ((128, 1), (512, 4), (2048, 16))
N_GROUPS_B = len(DILATED_GROUPS)
BLOCK = 128
NUM_BUCKETS = 32
MAX_DISTANCE = 2048
D_FF = ((8 * D_MODEL // 3 + 127) // 128) * 128
ALPHA = (2 * DEPTH) ** 0.25
BETA = (8 * DEPTH) ** -0.25
LN_EPS = 1e-5
NEG_INF = -1e30
N_LAYERS_A = (DEPTH + 1) // 2
N_LAYERS_B = DEPTH // 2
QKV_A = (N_HEADS + 2 * N_KV_HEADS_A) * HEAD_DIM
QKV_B = N_GROUPS_B * 3 * N_HEADS * HEAD_DIM
SCALE = HEAD_DIM ** -0.5

kernel_name = "hybrid_swa_sink_dilated_macaron_deepnorm_step"

def t5_bucket(dist):
    max_exact = NUM_BUCKETS // 2
    d = jnp.maximum(dist.astype(jnp.float32), 1.0)
    large = max_exact + (jnp.log(d / max_exact) / math.log(MAX_DISTANCE / max_exact)
                         * (NUM_BUCKETS - max_exact)).astype(jnp.int32)
    large = jnp.minimum(large, NUM_BUCKETS - 1)
    return jnp.where(dist < max_exact, dist, large)

def rel_bias(table, dist):
    return jnp.moveaxis(table.astype(jnp.float32)[t5_bucket(dist)], -1, 0)

def layer_norm(x, g, b):
    xf = x.astype(jnp.float32)
    mu = jnp.mean(xf, -1, keepdims=True)
    var = jnp.mean(jnp.square(xf - mu), -1, keepdims=True)
    y = (xf - mu) * lax.rsqrt(var + LN_EPS) * g.astype(jnp.float32) + b.astype(jnp.float32)
    return y.astype(x.dtype)

def swiglu(x, w_gate, w_up, w_down):
    return (jax.nn.silu(x @ w_gate) * (x @ w_up)) @ w_down

def masked_softmax(s, valid):
    s = jnp.where(valid, s, NEG_INF)
    m = jnp.max(s, -1, keepdims=True)
    e = jnp.exp(s - m)
    den = jnp.sum(e, -1, keepdims=True)
    return e / den, (m + jnp.log(den))[..., 0]

def banded_attention(q, k, v, n_invalid, window_units, dilation, table):
    n, L, hq, dh = q.shape
    hkv = k.shape[2]
    g = hq // hkv
    nb = L // BLOCK
    qb = q.reshape(n, nb, BLOCK, hkv, g, dh)

    def with_prev(t):
        t = t.reshape(n, nb, BLOCK, hkv, dh)
        prev = jnp.concatenate([jnp.zeros_like(t[:, :1]), t[:, :-1]], axis=1)
        return jnp.concatenate([prev, t], axis=2)

    k2, v2 = with_prev(k), with_prev(v)
    qi = jnp.arange(BLOCK)[:, None]
    ki = jnp.arange(2 * BLOCK)[None, :]
    rel = qi + BLOCK - ki
    band = (rel >= 0) & (rel <= window_units)
    key_unit = jnp.arange(nb)[:, None] * BLOCK + jnp.arange(2 * BLOCK)[None, :] - BLOCK
    valid = band[None] & (key_unit >= n_invalid)[:, None, :]
    bias = rel_bias(table, jnp.maximum(rel, 0) * dilation).reshape(hkv, g, BLOCK, 2 * BLOCK)
    s = jnp.einsum('nbqhgd,nbkhd->nbhgqk', qb, k2, preferred_element_type=jnp.float32) * SCALE + bias
    p, lse = masked_softmax(s, valid[None, :, None, None])
    o = jnp.einsum('nbhgqk,nbkhd->nbqhgd', p.astype(v.dtype), v2).reshape(n, L, hq, dh)
    lse = lse.transpose(0, 1, 4, 2, 3).reshape(n, L, hq)
    return o, lse

def gathered_attention(q, kv_cat, window_units, dilation, table):
    n, t, hq, dh = q.shape
    hkv = kv_cat.shape[3]
    g = hq // hkv
    lb = kv_cat.shape[1] - t
    j = jnp.arange(window_units + 1)
    idx = lb + jnp.arange(t)[:, None] - j[None, :] * dilation
    valid = idx >= 0
    kvg = kv_cat[:, jnp.maximum(idx, 0)]
    bias = rel_bias(table, j * dilation).reshape(hkv, g, -1)
    qg = q.reshape(n, t, hkv, g, dh)
    s = jnp.einsum('nthgd,ntjhd->nthgj', qg, kvg[:, :, :, 0], preferred_element_type=jnp.float32) * SCALE
    s = s + bias[None, None]
    p, lse = masked_softmax(s, valid[None, :, None, None, :])
    o = jnp.einsum('nthgj,ntjhd->nthgd', p.astype(kv_cat.dtype), kvg[:, :, :, 1]).reshape(n, t, hq, dh)
    return o, lse.reshape(n, t, hq)

def sink_gate(o, lse, sinks):
    return o * jax.nn.sigmoid(lse - sinks.astype(jnp.float32)).astype(o.dtype)[..., None]

def combine_groups(outs, lses):
    w = jax.nn.softmax(jnp.stack(lses, 0), axis=0)
    return jnp.einsum('gnth,gnthd->nthd', w.astype(outs[0].dtype), jnp.stack(outs, 0))

def mixer_a_prompt(x, w_qkv, w_o, sinks, table):
    b, s, _ = x.shape
    qkv = x @ w_qkv
    q = qkv[..., :N_HEADS * HEAD_DIM].reshape(b, s, N_HEADS, HEAD_DIM)
    kv = qkv[..., N_HEADS * HEAD_DIM:].reshape(b, s, 2, N_KV_HEADS_A, HEAD_DIM)
    o, lse = banded_attention(q, kv[:, :, 0], kv[:, :, 1], 0, WINDOW_A, 1, table)
    y = sink_gate(o, lse, sinks).reshape(b, s, -1) @ w_o
    keep = min(WINDOW_A, s)
    return y, kv[:, s - keep:]

def mixer_a_sample(x, cache, w_qkv, w_o, sinks, table):
    n, t, _ = x.shape
    qkv = x @ w_qkv
    q = qkv[..., :N_HEADS * HEAD_DIM].reshape(n, t, N_HEADS, HEAD_DIM)
    kv = qkv[..., N_HEADS * HEAD_DIM:].reshape(n, t, 2, N_KV_HEADS_A, HEAD_DIM)
    kv_cat = jnp.concatenate([cache.astype(kv.dtype), kv], axis=1)
    o, lse = gathered_attention(q, kv_cat, WINDOW_A, 1, table)
    y = sink_gate(o, lse, sinks).reshape(n, t, -1) @ w_o
    return y, kv_cat[:, t:]

def mixer_b_prompt(x, w_qkv, w_o, table):
    b, s, _ = x.shape
    qkv = (x @ w_qkv).reshape(b, s, N_GROUPS_B, 3, N_HEADS, HEAD_DIM)
    outs, lses, states = [], [], []
    for gi, (w, d) in enumerate(DILATED_GROUPS):
        span = d * BLOCK
        s_pad = -(-s // span) * span
        pad = s_pad - s
        lsub = s_pad // d

        def to_strided(t):
            t = jnp.pad(t, ((0, 0), (pad, 0), (0, 0), (0, 0)))
            t = t.reshape(b, lsub, d, N_HEADS, HEAD_DIM).transpose(0, 2, 1, 3, 4)
            return t.reshape(b * d, lsub, N_HEADS, HEAD_DIM)

        o, lse = banded_attention(to_strided(qkv[:, :, gi, 0]), to_strided(qkv[:, :, gi, 1]),
                                  to_strided(qkv[:, :, gi, 2]), pad // d, w // d, d, table)
        o = o.reshape(b, d, lsub, N_HEADS, HEAD_DIM).transpose(0, 2, 1, 3, 4).reshape(b, s_pad, N_HEADS, HEAD_DIM)
        lse = lse.reshape(b, d, lsub, N_HEADS).transpose(0, 2, 1, 3).reshape(b, s_pad, N_HEADS)
        outs.append(o[:, pad:])
        lses.append(lse[:, pad:])
        keep = min(w, s)
        states.append(qkv[:, s - keep:, gi, 1:3])
    y = combine_groups(outs, lses).reshape(b, s, -1) @ w_o
    return y, states

def mixer_b_sample(x, caches, w_qkv, w_o, table):
    n, t, _ = x.shape
    qkv = (x @ w_qkv).reshape(n, t, N_GROUPS_B, 3, N_HEADS, HEAD_DIM)
    outs, lses, states = [], [], []
    for gi, (w, d) in enumerate(DILATED_GROUPS):
        kv_cat = jnp.concatenate([caches[gi].astype(qkv.dtype), qkv[:, :, gi, 1:3]], axis=1)
        o, lse = gathered_attention(qkv[:, :, gi, 0], kv_cat, w // d, d, table)
        outs.append(o)
        lses.append(lse)
        states.append(kv_cat[:, t:])
    y = combine_groups(outs, lses).reshape(n, t, -1) @ w_o
    return y, states

def setup_inputs(seed: int = 0) -> dict:
    key = jax.random.key(seed)
    ks = jax.random.split(key, 20)
    f32 = jnp.float32
    nrm = lambda k, shape, scale: jax.random.normal(k, shape, f32) * scale
    lb_a = min(WINDOW_A, PAST_LEN)
    lb_b = [min(w, PAST_LEN) for (w, _) in DILATED_GROUPS]
    return {
        "x_prompt": nrm(ks[0], (BATCH, SEQ, D_MODEL), 1.0),
        "x_sample": nrm(ks[1], (DEC_BATCH, DEC_SEQ, D_MODEL), 1.0),
        "cache_a_kv": nrm(ks[2], (N_LAYERS_A, DEC_BATCH, lb_a, 2, N_KV_HEADS_A, HEAD_DIM), 1.0),
        "cache_b1_kv": nrm(ks[3], (N_LAYERS_B, DEC_BATCH, lb_b[0], 2, N_HEADS, HEAD_DIM), 1.0),
        "cache_b2_kv": nrm(ks[4], (N_LAYERS_B, DEC_BATCH, lb_b[1], 2, N_HEADS, HEAD_DIM), 1.0),
        "cache_b3_kv": nrm(ks[5], (N_LAYERS_B, DEC_BATCH, lb_b[2], 2, N_HEADS, HEAD_DIM), 1.0),
        "rel_bias_table": nrm(ks[6], (NUM_BUCKETS, N_HEADS), 0.3),
        "ln_gain": 1.0 + nrm(ks[7], (DEPTH, 3, D_MODEL), 0.02),
        "ln_bias": nrm(ks[8], (DEPTH, 3, D_MODEL), 0.02),
        "ffn_w_gate": nrm(ks[9], (DEPTH, 2, D_MODEL, D_FF), D_MODEL ** -0.5),
        "ffn_w_up": nrm(ks[10], (DEPTH, 2, D_MODEL, D_FF), D_MODEL ** -0.5),
        "ffn_w_down": nrm(ks[11], (DEPTH, 2, D_FF, D_MODEL), BETA * D_FF ** -0.5),
        "attn_a_w_qkv": nrm(ks[12], (N_LAYERS_A, D_MODEL, QKV_A), D_MODEL ** -0.5),
        "attn_a_w_o": nrm(ks[13], (N_LAYERS_A, N_HEADS * HEAD_DIM, D_MODEL), BETA * (N_HEADS * HEAD_DIM) ** -0.5),
        "attn_a_sinks": nrm(ks[14], (N_LAYERS_A, N_HEADS), 0.5),
        "attn_b_w_qkv": nrm(ks[15], (N_LAYERS_B, D_MODEL, QKV_B), D_MODEL ** -0.5),
        "attn_b_w_o": nrm(ks[16], (N_LAYERS_B, N_HEADS * HEAD_DIM, D_MODEL), BETA * (N_HEADS * HEAD_DIM) ** -0.5),
    }

def reference(x_prompt, x_sample, cache_a_kv, cache_b1_kv, cache_b2_kv, cache_b3_kv, rel_bias_table,
              ln_gain, ln_bias, ffn_w_gate, ffn_w_up, ffn_w_down, attn_a_w_qkv, attn_a_w_o,
              attn_a_sinks, attn_b_w_qkv, attn_b_w_o):
    def post_norm(x, delta, i, j):
        return layer_norm(ALPHA * x + delta, ln_gain[i, j], ln_bias[i, j])

    def half_ffn(x, i, f, j):
        return post_norm(x, 0.5 * swiglu(x, ffn_w_gate[i, f], ffn_w_up[i, f], ffn_w_down[i, f]), i, j)

    xp, xs = x_prompt, x_sample
    a_p, a_s = [], []
    b1_p, b2_p, b3_p, b1_s, b2_s, b3_s = [], [], [], [], [], []
    for i in range(DEPTH):
        li = i // 2
        xp, xs = half_ffn(xp, i, 0, 0), half_ffn(xs, i, 0, 0)
        if i % 2 == 0:
            yp, sp = mixer_a_prompt(xp, attn_a_w_qkv[li], attn_a_w_o[li], attn_a_sinks[li], rel_bias_table)
            ys, ss = mixer_a_sample(xs, cache_a_kv[li], attn_a_w_qkv[li], attn_a_w_o[li], attn_a_sinks[li], rel_bias_table)
            a_p.append(sp)
            a_s.append(ss)
        else:
            yp, sps = mixer_b_prompt(xp, attn_b_w_qkv[li], attn_b_w_o[li], rel_bias_table)
            ys, sss = mixer_b_sample(xs, (cache_b1_kv[li], cache_b2_kv[li], cache_b3_kv[li]),
                                     attn_b_w_qkv[li], attn_b_w_o[li], rel_bias_table)
            b1_p.append(sps[0]); b2_p.append(sps[1]); b3_p.append(sps[2])
            b1_s.append(sss[0]); b2_s.append(sss[1]); b3_s.append(sss[2])
        xp, xs = post_norm(xp, yp, i, 1), post_norm(xs, ys, i, 1)
        xp, xs = half_ffn(xp, i, 1, 2), half_ffn(xs, i, 1, 2)
    return (xp, xs,
            jnp.stack(a_p, 0), jnp.stack(b1_p, 0), jnp.stack(b2_p, 0), jnp.stack(b3_p, 0),
            jnp.stack(a_s, 0), jnp.stack(b1_s, 0), jnp.stack(b2_s, 0), jnp.stack(b3_s, 0))


_drawn_inputs = setup_inputs


def setup_inputs(seed=0):
    import zlib

    import numpy as np

    out = dict(_drawn_inputs(seed))
    spreads = {}
    factors = {'rel_bias_table': 2.83, 'attn_a_sinks': 8.0}
    for name, (base, spread) in spreads.items():
        noise = np.random.default_rng([zlib.crc32(name.encode()), seed]).standard_normal(out[name].shape)
        drawn = base * np.exp(spread * noise) if base else spread * noise
        out[name] = __import__('jax').numpy.asarray(drawn.astype(out[name].dtype))
    for name, factor in factors.items():
        out[name] = (out[name] * factor).astype(out[name].dtype)
    return out
```

```python
from contextlib import ExitStack

import numpy as np

import concourse.bass as bass
from concourse import mybir

F32 = mybir.dt.float32
F32R = mybir.dt.float32r
ALU = mybir.AluOpType
ACT = mybir.ActivationFunctionType
AX_X = mybir.AxisListType.X

P = 128
D_MODEL = 1024
KC = D_MODEL // P
SEQ = 512
NS = 8
DEC = 4
SAMPLE = NS * DEC
TOK = SEQ + SAMPLE
HALF = TOK // 2
D_FF = ((8 * D_MODEL // 3 + 127) // 128) * 128
FC = D_FF // P
FU = FC // 2
DEPTH = 2
HEADS = 16
HD = 64
PAIRS = HEADS // 2
KV_A = 4
ALPHA = (2 * DEPTH) ** 0.25
LN_EPS = 1e-5
SCALE = HD ** -0.5
NEG = -1e30
BLK = 128
NBLK = SEQ // BLK
DILATION = (1, 4, 16)
WINDOW = (128, 512, 2048)
NUM_BUCKETS = 32
MAX_DISTANCE = 2048
QKV_A = (HEADS + 2 * KV_A) * HD
RAW = 4
KV_SLOTS = 5
LINE_X, LINE_Y = 384, 256
LINES = LINE_X + 2 * LINE_Y
DEC_COLS = BLK


def bucket(dist):
    exact = NUM_BUCKETS // 2
    d = np.maximum(dist.astype(np.float32), np.float32(1.0))
    large = exact + (np.log(d / np.float32(exact)) / np.float32(np.log(MAX_DISTANCE / exact))
                     * np.float32(NUM_BUCKETS - exact)).astype(np.int32)
    return np.where(dist < exact, dist, np.minimum(large, NUM_BUCKETS - 1))


def one_hot_lines():
    out = np.zeros((NUM_BUCKETS + 1, LINES), np.float32)

    def put(col, dist, valid):
        b = bucket(np.maximum(dist, 0))
        for c, bb, ok in zip(col, b, valid):
            if ok:
                out[bb, c] = 1.0
            else:
                out[NUM_BUCKETS, c] = NEG
    j = np.arange(LINE_X)
    rel = 2 * BLK - 1 - j
    put(j, rel, (rel >= 0) & (rel <= BLK))
    j = np.arange(LINE_Y)
    rel = BLK - 1 - j
    put(LINE_X + j, rel * 4, rel >= 0)
    put(LINE_X + LINE_Y + j, rel * 4, (rel >= 0) & (rel % 4 == 0))
    return out


def one_hot_decode():
    n0 = BLK + DEC - 1
    out = np.zeros((NUM_BUCKETS + 1, n0 + 2 * BLK + 2 * DEC), np.float32)

    def put(c, dist, ok):
        if ok:
            out[int(bucket(np.array([dist]))[0]), c] = 1.0
        else:
            out[NUM_BUCKETS, c] = NEG
    for j in range(n0):
        dist = BLK - (j - (DEC - 1))
        put(j, dist, 0 <= dist <= BLK)
    for g in (1, 2):
        for i in range(BLK):
            put(n0 + (g - 1) * BLK + i, (BLK - i) * DILATION[g], True)
    for j in range(2 * DEC - 1):
        dist = DEC - 1 - j
        put(n0 + 2 * BLK + j, dist, dist >= 0)
    put(n0 + 2 * BLK + 2 * DEC - 1, 0, True)
    return out


def build(nc, t, o):
    oh_lines, oh_dec = t["c_lines"], t["c_dec"]
    ND = oh_dec.shape[1]
    N0 = BLK + DEC - 1
    with ExitStack() as ctx:
        def sem(name):
            return ctx.enter_context(nc.semaphore(name))

        def sb(name, shape, dt=F32, scope=None):
            return (scope or ctx).enter_context(nc.sbuf_tensor("sb_" + name, shape, dt))

        def dram(name, shape):
            return nc.dram_tensor("scr_" + name, shape, F32, kind="Internal").ap()

        lines_d = [dram("lines_x", [HEADS, P, LINE_X]), dram("lines_y0", [HEADS, P, LINE_Y]), dram("lines_y1", [HEADS, P, LINE_Y])]
        dec_lines_d = dram("dec_lines", [HEADS, ND])
        q_d = {0: dram("qa", [SAMPLE, 1, D_MODEL]), 1: dram("qb", [SAMPLE, 3, D_MODEL])}
        kv_d = {0: dram("kva", [SAMPLE, 1, 2, KV_A * HD]), 1: dram("kvb", [SAMPLE, 3, 2, D_MODEL])}
        md_d = dram("md", [2, 2, SEQ, 2 * PAIRS])
        snew_d = {0: dram("snew_a", [SAMPLE * HEADS, DEC]), 1: dram("snew_b", [SAMPLE * HEADS, DEC + 2])}
        pnew_d = {0: dram("pnew_a", [SAMPLE * HEADS, DEC]), 1: dram("pnew_b", [SAMPLE * HEADS, DEC + 2])}
        odec_d = {0: dram("odec_a", [SAMPLE, D_MODEL]), 1: dram("odec_b", [SAMPLE, D_MODEL])}

        z = sb("z", [P, KC, TOK])
        xh = sb("xh", [P, KC, TOK], F32R)
        xl = sb("xl", [P, KC, TOK], F32R)
        raw = [sb(f"raw{i}", [P, FU, P]) for i in range(RAW)]
        wh = [sb(f"wh{i}", [P, FU, P], F32R) for i in range(2)]
        wl = [sb(f"wl{i}", [P, FU, P], F32R) for i in range(2)]
        ident = sb("ident", [P, P])
        ones = sb("ones", [P, P])
        pick32 = sb("pick32", [P, SAMPLE])
        pick = sb("pick", [P, SAMPLE], F32R)
        gain = sb("gain", [P, 3 * DEPTH, KC])
        shift = sb("shift", [P, 3 * DEPTH, KC])
        rstd = sb("rstd", [P, TOK])

        with ExitStack() as s:
            hh = sb("hh", [P, FC, TOK], F32R, s)
            hl = sb("hl", [P, FC, TOK], F32R, s)
            sil = [sb(f"sil{i}", [P, TOK], F32, s) for i in range(2)]
            h32 = [sb(f"h32{i}", [P, TOK], F32, s) for i in range(2)]
        with ExitStack() as s:
            sq = sb("sq", [P, KC, TOK], F32, s)
        with ExitStack() as s:
            xin = sb("xin", [P, NBLK, D_MODEL], F32, s)
            xsin = sb("xsin", [SAMPLE, D_MODEL], F32, s)
            tab = sb("tab", [NUM_BUCKETS + 1, HEADS], F32, s)
            oh1 = sb("oh1", [NUM_BUCKETS + 1, LINES], F32, s)
            oh2 = sb("oh2", [NUM_BUCKETS + 1, ND], F32, s)
            lin1 = sb("lin1", [HEADS, LINES], F32, s)
            lin2 = sb("lin2", [HEADS, ND], F32, s)
        with ExitStack() as s:
            yout = sb("yout", [P, NBLK + 1, D_MODEL], F32, s)

        def attn_common(s, n, heads):
            r = {}
            r["st"] = [sb(f"st{n}{i}", [P, TOK], F32, s) for i in range(2)]
            r["kt"] = [sb(f"kt{n}{i}", [P, NBLK * P], F32, s) for i in range(2)]
            r["ss"] = [sb(f"ss{n}{i}", [SAMPLE, P], F32, s) for i in range(2)]
            r["qs"] = [sb(f"qs{n}{i}", [P, 4, P], F32, s) for i in range(2)]
            r["bias"] = sb(f"bias{n}", [P, heads, 2 * BLK], F32, s)
            for m in ("nm", "dn"):
                r[m] = [sb(f"{m}{n}{i}", [P, 2], F32, s) for i in range(2)]
            return r

        with ExitStack() as s:
            RA = attn_common(s, "a", HEADS)
            RA["q"] = [sb("qa", [P, PAIRS, SEQ], F32, s)]
            RA["k"] = [sb("ka", [P, 2, SEQ], F32, s)]
            RA["v"] = [sb("va", [P, NBLK, KV_A * HD], F32, s)]
            RA["o"] = [sb("oa", [P, NBLK, HEADS * HD], F32, s)]
            RA["md"] = [sb("mda", [P, NBLK, 2, HEADS], F32, s)]
            RA["mo"] = [sb("moa", [P, NBLK, 2, HEADS], F32, s)]
            RA["sink"] = sb("sinka", [P, HEADS], F32, s)
            RA["t"] = [sb(f"ta{i}", [P, NBLK, HEADS], F32, s) for i in range(5)]
        with ExitStack() as s:
            RB = attn_common(s, "b", PAIRS)
            for m in ("q", "k"):
                RB[m] = [sb(f"{m}b{i}", [P, 4, SEQ], F32, s) for i in range(2)]
            RB["v"] = [sb(f"vb{i}", [P, NBLK, SEQ], F32, s) for i in range(2)]
            RB["o"] = [sb(f"ob{i}", [P, NBLK, SEQ], F32, s) for i in range(2)]
            RB["md"] = [sb(f"mdb{i}", [P, NBLK, 2, PAIRS], F32, s) for i in range(2)]
            RB["mo"] = [sb(f"mob{i}", [P, NBLK, 2, PAIRS], F32, s) for i in range(2)]
            RB["t"] = [sb(f"tb{i}", [P, NBLK, PAIRS], F32, s) for i in range(5)]
            RB["at"] = sb("at", [P, 4, SEQ], F32, s)

        def decode_regime(s, n, G, kv, new):
            r = {}
            r["kv"] = [sb(f"dkv{n}{i}", [P, kv * HD], F32, s) for i in range(KV_SLOTS)]
            r["qb"] = [sb(f"dqb{n}{i}", [P, D_MODEL], F32, s) for i in range(3)]
            r["pr"] = [sb(f"dpr{n}{i}", [P, D_MODEL], F32, s) for i in range(3)]
            r["s"] = sb(f"ds{n}", [P, G, SAMPLE * HEADS], F32, s)
            r["p"] = sb(f"dp{n}", [P, G, SAMPLE, 32], F32, s)
            r["sm"] = [sb(f"dsm{n}{i}", [P, G * P + new + 1], F32, s) for i in range(2)]
            r["bc"] = sb(f"dbc{n}", [P, G, P], F32, s)
            r["bn"] = sb(f"dbn{n}", [P, new], F32, s)
            r["snk"] = sb(f"dsnk{n}", [P, 1], F32, s)
            r["snew"] = sb(f"dsn{n}", [SAMPLE, HEADS, new], F32, s)
            r["snb"] = sb(f"dsnb{n}", [P, 4, new], F32, s)
            r["pnb"] = sb(f"dpnb{n}", [P, 4, new], F32, s)
            r["pn"] = sb(f"dpn{n}", [SAMPLE, HEADS, new], F32, s)
            r["st"] = sb(f"dst{n}", [P, 4, 4], F32, s)
            r["qn"] = sb(f"dqn{n}", [2 * SAMPLE, G, D_MODEL], F32, s)
            r["q2"] = sb(f"dq2{n}", [P, G, D_MODEL], F32R, s)
            r["kn"] = [sb(f"dkn{n}{i}", [SAMPLE, kv * HD], F32, s) for i in range(2)]
            r["mask"] = sb(f"dmask{n}", [P, kv], F32, s)
            r["oc"] = sb(f"doc{n}", [P, NS, HD], F32, s)
            r["ot"] = sb(f"dot{n}", [SAMPLE, D_MODEL], F32, s)
            return r
        with ExitStack() as s:
            DA = decode_regime(s, "a", 1, KV_A, DEC)
        with ExitStack() as s:
            DB = decode_regime(s, "b", 3, HEADS, DEC + 2)

        bank = [ctx.enter_context(nc.psum_tensor(f"bank{i}", [P, 512], F32)) for i in range(8)]

        raw_in = [sem(f"raw_in{i}") for i in range(RAW)]
        wh_rdy, wl_rdy = sem("wh_rdy"), sem("wl_rdy")
        mm_done = sem("mm_done")
        acc_free = [sem(f"acc_free{i}") for i in range(2)]
        hh_rdy, hl_rdy = sem("hh_rdy"), sem("hl_rdy")
        ln_mean, ln_dev, ln_sq, ln_var, ln_rs, ln_nrm = (sem("ln_" + n) for n in ("mean", "dev", "sq", "var", "rs", "nrm"))
        ln_aff, x_hi, x_lo, ln_ax = (sem(n) for n in ("ln_aff", "x_hi", "x_lo", "ln_ax"))
        in_ld, cst_ld, setup, init_t, line_t, line_c, line_o = (
            sem(n) for n in ("in_ld", "cst_ld", "setup", "init_t", "line_t", "line_c", "line_o"))
        tr_done = sem("tr_done")
        tr_free = [sem(f"tr_free{i}") for i in range(2)]
        qk_cp = sem("qk_cp")
        kt_out = [sem(f"kt_out{i}") for i in range(2)]
        ss_out = [sem(f"ss_out{i}") for i in range(2)]
        v_out = sem("v_out")
        qs_zero, qs_rdy = sem("qs_zero"), sem("qs_rdy")
        sc_done, sm_done, nm_done, ex_done, pt_done, ptc_done, pv_done, oev_done = (
            sem(n) for n in ("sc_done", "sm_done", "nm_done", "ex_done", "pt_done", "ptc_done", "pv_done", "oev_done"))
        bias_ld, md_out, md_in, cmb_v, cmb_a, cmb_r, ow_rdy, st_done, sink_rdy, d_sx, d_sum, ln_root = (
            sem(n) for n in ("bias_ld", "md_out", "md_in", "cmb_v", "cmb_a", "cmb_r", "ow_rdy", "st_done", "sink_rdy", "d_sx", "d_sum", "ln_root"))
        ot_done, ot_a, ot_v, sp_h, sp_l = (sem(n) for n in ("ot_done", "ot_a", "ot_v", "sp_h", "sp_l"))
        d_kv = [sem(f"d_kv{i}") for i in range(KV_SLOTS)]
        d_qp, d_qb = sem("d_qp"), sem("d_qb")
        d_mult = [sem("d_mult_pool"), sem("d_mult_dve")]
        d_kn = [sem(f"d_kn{i}") for i in range(2)]
        (d_cst, d_qn, d_q2, d_red, d_nv, d_sn_out, d_sn_in, d_st, d_sv, d_nm, d_ex, d_pt, d_ptc, d_pn_out, d_pn_in,
         d_pv, d_msk, d_oc, d_oc_out, d_ot_in, d_tt, d_ta, d_tv, d_zero) = (
            sem("d_" + n) for n in ("cst", "qn", "q2", "red", "nv", "sn_out", "sn_in", "st", "sv", "nm", "ex", "pt",
                                    "ptc", "pn_out", "pn_in", "pv", "msk", "oc", "oc_out", "ot_in", "tt", "ta",
                                    "tv", "zero"))
        out_t, out_ca, out_cv, out_done, new_done = (sem(n) for n in ("out_t", "out_ca", "out_cv", "out_done", "new_done"))
        copy_done = [sem(f"copy_done{i}") for i in range(5)]

        class Phase:
            def __init__(self, kind, units, chunks, dmas=1, l=None, f=None, ffn=None):
                self.kind, self.units, self.chunks, self.dmas = kind, units, chunks, dmas
                self.l, self.f, self.ffn = l, f, ffn

        phases = []

        def add(*a, **kw):
            ph = Phase(*a, **kw)
            if phases:
                q = phases[-1]
                q.next = ph
                ph.u0, ph.t0 = q.u0 + q.units, q.t0 + q.tiles
                ph.land0 = [x + 16 * q.dmas * (q.units // RAW) for x in q.land0]
            else:
                ph.u0, ph.t0, ph.land0 = 0, 0, [0] * RAW
            ph.tiles = ph.units // 2 if ph.kind == "down" else ph.units
            ph.next = None
            phases.append(ph)
            return ph

        up, down, qkv, wo = {}, {}, {}, {}
        for l in range(DEPTH):
            for f in range(2):
                up[l, f] = add("up", 2 * FC, KC, l=l, f=f, ffn=2 * l + f)
                down[l, f] = add("down", 2 * KC, FU, l=l, f=f, ffn=2 * l + f)
                if f == 0 and l == 0:
                    qkv[0] = add("qkv", 12, KC, dmas=2)
                    wo[0] = add("wo", KC, KC, dmas=4)
                elif f == 0:
                    for r in range(2):
                        qkv[1, r, 0] = add("qkv", 12, KC)
                        qkv[1, r, 1] = add("qkv", 24, KC)
                    wo[1] = add("wo", KC, KC)

        def acc(s, h):
            return bank[2 * s + h][:, 0:HALF]

        halves = [slice(0, HALF), slice(HALF, TOK)]

        class Run:
            pass
        runs = []

        def add_run(ph, layer, rnd, groups):
            r = Run()
            r.ph, r.layer, r.rnd, r.n = ph, layer, rnd, ph.units
            r.tr0 = sum(x.n for x in runs)
            r.td0 = r.tr0 + len(runs)
            r.items = []
            for gi, g in enumerate(groups):
                for kind, cnt in (("q", PAIRS if layer == 0 else 4), ("k", 2 if layer == 0 else 4),
                                  ("v", 2 if layer == 0 else 4)):
                    r.items += [(gi, g, kind, p) for p in range(cnt)]
            r.R = RA if layer == 0 else RB
            runs.append(r)
            ph.run = r
            return r
        run_a = add_run(qkv[0], 0, 0, [0])
        run_b = [[add_run(qkv[1, r, 0], 1, r, [0]), add_run(qkv[1, r, 1], 1, r, [1, 2])] for r in range(2)]

        class Pass:
            def __init__(self, n, R, pairs, first, dilated, slot):
                self.n, self.R, self.pairs, self.u0, self.dilated, self.slot = n, R, pairs, first, dilated, slot
                self.units = 4 * pairs
        pass_a = Pass(0, RA, PAIRS, 0, False, 0)
        pass_b = []
        nu = pass_a.units
        for r in range(2):
            for y in range(2):
                pass_b.append(Pass(1 + 2 * r + y, RB, 4, nu, bool(y), y))
                nu += 16

        def skewed(eng, n_pairs, stages):
            last = max(lag for _, lag in stages)
            for s_ in range(4):
                for fn, lag in stages:
                    if s_ >= lag:
                        fn(0, s_ - lag)
            with eng.Fori(1, n_pairs) as i:
                for s_ in range(4):
                    for fn, lag in stages:
                        fn(i + (s_ - lag) // 4, (s_ - lag) % 4)
            for s_ in range(last):
                for fn, lag in stages:
                    if s_ < lag:
                        fn(n_pairs - 1, 4 + s_ - lag)

        def first_col(ps, blk):
            return BLK if (not ps.dilated and blk == 0) else 0

        LAYER = {0: dict(G=1, kv=KV_A, new=DEC, D=DA, ps=pass_a, runs=[run_a]),
                 1: dict(G=3, kv=HEADS, new=DEC + 2, D=DB, ps=pass_b[-1], runs=run_b[0] + run_b[1])}
        caches = {(0, 0): t["cache_a_kv"], (1, 0): t["cache_b1_kv"], (1, 1): t["cache_b2_kv"], (1, 2): t["cache_b3_kv"]}
        states_p = {(0, 0): o["state_a_p"], (1, 0): o["state_b1_p"], (1, 1): o["state_b2_p"], (1, 2): o["state_b3_p"]}
        states_s = {(0, 0): o["state_a_s"], (1, 0): o["state_b1_s"], (1, 1): o["state_b2_s"], (1, 2): o["state_b3_s"]}

        count = {"kt": [0, 0], "ss": [0, 0], "cp": 0, "v": 0}
        for r in runs:
            r.kt_before, r.ss_before, r.cp_after, r.cp0 = [], [], [], count["cp"]
            for i, (gi, g, kind, p_) in enumerate(r.items):
                b = i % 2
                r.kt_before.append(count["kt"][b])
                r.ss_before.append(count["ss"][b])
                count["ss"][b] += 16
                if kind == "k":
                    count["kt"][b] += 16
                if kind == "v":
                    count["v"] += 16
                else:
                    count["cp"] += 1
                r.cp_after.append(count["cp"])
            r.kt_total, r.ss_total, r.v_total, r.cp_total = list(count["kt"]), list(count["ss"]), count["v"], count["cp"]

        def new_cols(layer):
            c = [(0, t_) for t_ in range(DEC)]
            return c if layer == 0 else c + [(1, None), (2, None)]

        def dec_tiles(layer):
            out = []
            for n in range(NS):
                out.append((n, 0, tuple(range(DEC))))
                for g in range(1, LAYER[layer]["G"]):
                    out += [(n, g, (tau,)) for tau in range(DEC)]
            return out

        class Load:
            def __init__(self, ring, slots, what):
                self.i = len(ring)
                self.slot = self.i % slots
                self.val = 16 * (self.i // slots + 1)
                self.landed = None
                self.what = what
                self.done = None
                self.prev = ring[self.i - slots] if self.i >= slots else None
                ring.append(self)

        class Product:
            def __init__(self, k, n, g, tau, tile, mult):
                self.k, self.slot, self.n, self.g, self.tau, self.tile = k, k % 3, n, g, tau, tile
                self.by = int(self.slot == 2)
                mult[self.by] += 1
                self.mult = (d_mult[self.by], mult[self.by])

        kv_ring, kn_ring = [], []
        mult = [0, 0]
        n_prod = n_pv = n_nv = 0
        for layer in range(2):
            L = LAYER[layer]
            L["kn"], L["k"], L["prod"], L["v"], L["vn"] = [], [], [], [], []
            L["nv0"] = n_nv
            for c_, (g, tp) in enumerate(new_cols(layer)):
                x = Load(kn_ring, 2, (c_, g, tp))
                n_nv += 2
                x.done = [(d_nv, n_nv)]
                L["kn"].append(x)
            for n, g, taus in dec_tiles(layer):
                x = Load(kv_ring, KV_SLOTS, (n, g, taus))
                L["k"].append(x)
                x.prods = []
                for tau in taus:
                    x.prods.append(Product(n_prod, n, g, tau, x, mult))
                    n_prod += 1
                L["prod"] += x.prods
                x.done = [(d_mult[e], mult[e]) for e in range(2) if mult[e]]
            for n, g, taus in dec_tiles(layer):
                x = Load(kv_ring, KV_SLOTS, (n, g, taus))
                n_pv += 1
                x.done = [(d_pv, n_pv)]
                L["v"].append(x)
            for c_, (g, tp) in enumerate(new_cols(layer)):
                x = Load(kn_ring, 2, (c_, g, tp))
                n_nv += 2
                x.done = [(d_nv, n_nv)]
                L["vn"].append(x)
        landed_ = [0, 0]
        for x in kn_ring:
            landed_[x.slot] += 16 * (1 if x.what[2] is None else NS)
            x.landed = landed_[x.slot]
        BIAS_LD = {0: 16 * 8}
        for ps in pass_b:
            BIAS_LD[ps.n] = BIAS_LD[ps.n - 1] + (32 if ps.dilated else 16)
        PASS_OF = [pass_a] + pass_b
        cst_dmas = {0: 3 * 2 * DEC + 1, 1: 5 * 2 * DEC + 1}

        UP_ITS, DOWN_ITS = 2 * FC // RAW, 2 * KC // RAW
        B3_KEEP, B2_KEEP = DILATION[2] * BLK - DEC, DILATION[1] * BLK - DEC
        UP_ROWS = 88
        DOWN_ROWS = (B3_KEEP - UP_ITS * 2 * UP_ROWS) // DOWN_ITS
        B2_ROWS = B2_KEEP // DOWN_ITS
        assert UP_ITS * 2 * UP_ROWS + DOWN_ITS * DOWN_ROWS == B3_KEEP and DOWN_ITS * B2_ROWS == B2_KEEP

        def norm_index(layer, j):
            return 3 * layer + j

        block = ctx.enter_context(nc.Block())

        @block.sync
        def _(sp):
            sp.dma_start(ident[:], t["c_ident"]).then_inc(cst_ld, 16)
            sp.dma_start(pick32[:], t["c_pick"]).then_inc(cst_ld, 16)
            sp.dma_start(tab[0:NUM_BUCKETS, :], t["rel_bias_table"]).then_inc(cst_ld, 16)
            sp.dma_start(oh1[:], oh_lines).then_inc(cst_ld, 16)
            sp.dma_start(oh2[:], oh_dec).then_inc(cst_ld, 16)
            with nc.allow_non_contiguous_dma(reason="feature on partition, a few values each"):
                for n_ in range(3 * DEPTH):
                    sp.dma_start(gain[:, n_, :], t["ln_gain"][n_ // 3, n_ % 3].rearrange("(c p) -> p c", p=P)).then_inc(cst_ld, 16)
                    sp.dma_start(shift[:, n_, :], t["ln_bias"][n_ // 3, n_ % 3].rearrange("(c p) -> p c", p=P)).then_inc(cst_ld, 16)
            sp.dma_start(xin[:], t["x_prompt"][0].rearrange("(b p) d -> p b d", p=P)).then_inc(in_ld, 16)
            sp.dma_start(xsin[:], t["x_sample"].rearrange("n t d -> (n t) d")).then_inc(in_ld, 16)

            def keep_rows(g, n, r0, rows, f):
                src = caches[1, g][0, n].rearrange("r w h d -> r (w h d)")[bass.ds(r0 + DEC, rows), :]
                dst = states_s[1, g][0, n].rearrange("r w h d -> r (w h d)")[bass.ds(r0, rows), :]
                sp.dma_start(dst, src).then_inc(copy_done[f], 16)

            def keep_small(layer, n0, n1):
                src = caches[layer, 0][0, n0:n1].rearrange("n r w h d -> n (r w h d)")
                dst = states_s[layer, 0][0, n0:n1].rearrange("n r w h d -> n (r w h d)")
                row = 2 * LAYER[layer]["kv"] * HD
                total = src.shape[1]
                sp.dma_start(dst[:, 0:total - DEC * row], src[:, DEC * row:total]).then_inc(copy_done[2 * DEPTH], 16)

            def load_unit(ph, it, j):
                sp.wait_ge(wl_rdy, it * RAW + (ph.u0 + j + 1))
                if ph.kind == "up":
                    w = t["ffn_w_gate" if j % 2 == 0 else "ffn_w_up"][ph.l, ph.f]
                    src = w.rearrange("(c p) (f n) -> p c f n", p=P, n=P)[:, :, bass.ds(it * 2 + j // 2, 1), :]
                    sp.dma_start(raw[j][:, 0:KC, :], src.rearrange("p c f n -> p c (f n)")).then_inc(raw_in[j], 16)
                elif ph.kind == "down":
                    w = t["ffn_w_down"][ph.l, ph.f].rearrange("(u c p) (m n) -> p u c m n", p=P, n=P, u=2)
                    src = w[:, j % 2, :, bass.ds(it * 2 + j // 2, 1), :]
                    sp.dma_start(raw[j][:], src.rearrange("p c m n -> p c (m n)")).then_inc(raw_in[j], 16)
                elif ph.kind == "qkv":
                    r = ph.run
                    w = t["attn_b_w_qkv"][0].rearrange("(c p) (k r j n) -> p c k r j n", p=P, r=2, j=4, n=P)
                    src = w[:, :, bass.ds(it + 3 * r.items[0][1], 1), r.rnd, j, :]
                    sp.dma_start(raw[j][:, 0:KC, :], src.rearrange("p c k n -> p c (k n)")).then_inc(raw_in[j], 16)
                elif ph.dmas == 1:
                    w = t["attn_b_w_o"][0].rearrange("(c p) (m n) -> p c m n", p=P, n=P)
                    src = w[:, :, bass.ds(it * RAW + j, 1), :]
                    sp.dma_start(raw[j][:, 0:KC, :], src.rearrange("p c m n -> p c (m n)")).then_inc(raw_in[j], 16)
                else:
                    w = t["attn_a_w_o"][0].rearrange("(g h r d) (m n) -> g h d r m n", g=2, h=2, d=HD, n=P)
                    for g in range(2):
                        for h in range(2):
                            src = w[g, h][:, :, bass.ds(it * RAW + j, 1), :].rearrange("d r m n -> d r (m n)")
                            sp.dma_start(raw[j][h * HD:(h + 1) * HD, 4 * g:4 * g + 4, :], src).then_inc(raw_in[j], 16)

            def load_units(ph, first):
                with sp.Fori(first, ph.units // RAW) as it:
                    for j in range(RAW):
                        load_unit(ph, it, j)
                        if ph.kind == "up":
                            keep_rows(2, 2 * ph.ffn + j % 2, it * (2 * UP_ROWS) + (j // 2) * UP_ROWS, UP_ROWS, ph.ffn)
                        elif ph.kind == "down" and j < 2:
                            keep_rows(1, 2 * ph.ffn + j % 2, it * B2_ROWS, B2_ROWS, ph.ffn)
                        elif ph.kind == "down":
                            keep_rows(2, 2 * ph.ffn + j % 2, it * DOWN_ROWS + UP_ITS * 2 * UP_ROWS, DOWN_ROWS, ph.ffn)

            def load_first(ph):
                for j in range(RAW):
                    load_unit(ph, 0, j)

            def load_qkv_a(ph, units):
                w = t["attn_a_w_qkv"][0].rearrange("(c p) n -> p c n", p=P)
                for i in units:
                    gi, g, kind, p_ = ph.run.items[i]
                    sp.wait_ge(wl_rdy, ph.u0 + i + 1)
                    for h in range(2):
                        if kind == "q":
                            col = ((p_ // 4) * 8 + h * 4 + p_ % 4) * HD
                        else:
                            col = (HEADS + (KV_A if kind == "v" else 0) + 2 * p_ + h) * HD
                        sp.dma_start(raw[i % RAW][:, 0:KC, h * HD:(h + 1) * HD], w[:, :, col:col + HD]).then_inc(raw_in[i % RAW], 16)

            def load_bias(ps):
                R = ps.R

                def toeplitz(l, h0, n, width):
                    W = lines_d[l].shape[2]
                    return bass.AP(lines_d[l].tensor, h0 * P * W + BLK - 1, [[W - 1, P], [P * W, n], [1, width]])

                if ps is pass_a or ps is pass_b[0]:
                    sp.wait_ge(ln_var, 2 * (norm_index(0 if ps is pass_a else 1, 0) + 1))
                else:
                    sp.wait_ge(sm_done, ps.u0 + 2)
                if ps is pass_a:
                    sp.wait_ge(line_o, 64)
                    for g in range(2):
                        for h in range(2):
                            dst = R["bias"][:].rearrange("p (g r h) k -> p g h r k", g=2, h=2)[:, g, h]
                            sp.dma_start(dst, toeplitz(0, g * 8 + h * 4, 4, 2 * BLK)).then_inc(bias_ld, 16)
                            with nc.allow_non_contiguous_dma(reason="4 sinks"):
                                dst = R["sink"][:].rearrange("p (g r h) -> p g h r", g=2, h=2)[:, g, h]
                                src = t["attn_a_sinks"][0:1, g * 8 + h * 4:g * 8 + h * 4 + 4]
                                sp.dma_start(dst, src.to_broadcast([P, 4])).then_inc(bias_ld, 16)
                else:
                    h0 = (ps.n - 1) // 2 * 8
                    if not ps.dilated:
                        sp.dma_start(R["bias"][:], toeplitz(0, h0, 8, 2 * BLK)).then_inc(bias_ld, 16)
                    else:
                        for g in range(2):
                            sp.dma_start(R["bias"][:, :, g * BLK:(g + 1) * BLK], toeplitz(1 + g, h0, 8, BLK)).then_inc(bias_ld, 16)

            def cached(layer, n, g, tau, which):
                c = caches[layer, g][0, n]
                if g == 0:
                    return c[:, which].rearrange("r h d -> r (h d)")
                return c.rearrange("(i e) w h d -> e i w (h d)", e=DILATION[g])[tau, :, which]

            def slot_free(x):
                if x.prev:
                    for s_, val in x.prev.done:
                        sp.wait_ge(s_, val)

            def load_new(layer, x, which):
                D, (c_, g, tp) = LAYER[layer]["D"], x.what
                slot_free(x)
                dst = D["kn"][x.slot][:]
                if tp is None:
                    sp.dma_start(dst, kv_d[layer][:, g, which, :]).then_inc(d_kn[x.slot], 16)
                else:
                    for n in range(NS):
                        src = kv_d[layer][n * DEC + tp:n * DEC + tp + 1, g, which, :]
                        sp.dma_start(dst[n * DEC:(n + 1) * DEC, :], src.to_broadcast([DEC, dst.shape[1]])).then_inc(d_kn[x.slot], 16)

            def load_decode_constants(layer):
                D = LAYER[layer]["D"]
                with nc.allow_non_contiguous_dma(reason="one value per partition"):
                    for tau in range(DEC):
                        for n2 in range(2):
                            rows = slice((n2 * DEC + tau) * HEADS, (n2 * DEC + tau + 1) * HEADS)
                            c0 = DEC - 1 - tau
                            sp.dma_start(D["bc"][rows, 0, :], dec_lines_d[:, c0:c0 + BLK]).then_inc(d_cst, 16)
                            c0 += N0 + 2 * BLK
                            sp.dma_start(D["bn"][rows, 0:DEC], dec_lines_d[:, c0:c0 + DEC]).then_inc(d_cst, 16)
                            if layer:
                                src = dec_lines_d[:, N0:N0 + 2 * BLK].rearrange("h (g r) -> h g r", g=2)
                                sp.dma_start(D["bc"][rows, 1:3, :], src).then_inc(d_cst, 16)
                                for c_ in range(2):
                                    sp.dma_start(D["bn"][rows, DEC + c_:DEC + c_ + 1], dec_lines_d[:, ND - 1:ND]).then_inc(d_cst, 16)
                            else:
                                sp.dma_start(D["snk"][rows, :], t["attn_a_sinks"].rearrange("o h -> h o")).then_inc(d_cst, 16)
                sp.dma_start(D["mask"][:], t["c_mask_b" if layer else "c_mask_a"]).then_inc(d_cst, 16)

            def load_decode(layer):
                L = LAYER[layer]
                D = L["D"]
                sp.wait_ge(d_zero, 2 * layer + 1)
                for k in range(2):
                    sp.dma_start(D["qn"][k * SAMPLE:(k + 1) * SAMPLE], q_d[layer]).then_inc(d_qn, 16)
                for m, x in enumerate(L["k"]):
                    n, g, taus = x.what
                    slot_free(x)
                    sp.dma_start(D["kv"][x.slot][:], cached(layer, n, g, taus[0], 0)).then_inc(d_kv[x.slot], 16)
                    if 1 <= m < 1 + len(L["kn"]):
                        load_new(layer, L["kn"][m - 1], 0)
                    if m == 1 + len(L["kn"]):
                        load_decode_constants(layer)
                for x in L["v"]:
                    n, g, taus = x.what
                    slot_free(x)
                    sp.dma_start(D["kv"][x.slot][:], cached(layer, n, g, taus[0], 1)).then_inc(d_kv[x.slot], 16)
                for x in L["vn"]:
                    load_new(layer, x, 1)

            peeled = 0
            for ph in phases:
                if ph is qkv[0]:
                    load_qkv_a(ph, range(RAW))
                    load_bias(pass_a)
                    load_qkv_a(ph, range(RAW, ph.units))
                elif ph.kind == "qkv":
                    if not peeled:
                        load_first(ph)
                    load_bias(pass_b[2 * ph.run.rnd + (ph.run.items[0][1] > 0)])
                    n0 = 4 * ph.run.rnd + 2 * (ph.run.items[0][1] > 0)
                    keep_small(1, n0, n0 + 2)
                    keep_small(0, n0, n0 + 2)
                    load_units(ph, 1)
                else:
                    load_units(ph, peeled)
                peeled = int(ph.kind == "qkv")
                if peeled:
                    load_first(ph.next)
                if ph is qkv[0]:
                    load_decode(0)
                if ph is qkv[1, 1, 1]:
                    load_decode(1)
            for f in range(2 * DEPTH):
                sp.wait_ge(copy_done[f], 16 * RAW * (UP_ITS + DOWN_ITS))
            sp.wait_ge(copy_done[2 * DEPTH], 16 * 2 * 4)
            sp.wait_ge(new_done, 16 * 4)
            sp.wait_ge(v_out, count["v"])
            for b in range(2):
                sp.wait_ge(kt_out[b], count["kt"][b])
                sp.wait_ge(ss_out[b], count["ss"][b])
            sp.wait_ge(out_done, 32)

        @block.tensor
        def _(pe):
            def gemm(slot, chunks, hi, lo, s, start, stop):
                for k in range(chunks):
                    for h in range(2):
                        a = acc(s, h)
                        pe.matmul(a, wl[slot][:, k, :], hi(k)[:, halves[h]], start=start and k == 0, stop=False)
                        pe.matmul(a, wh[slot][:, k, :], lo(k)[:, halves[h]], start=False, stop=False)
                        last = pe.matmul(a, wh[slot][:, k, :], hi(k)[:, halves[h]], start=False, stop=stop and k == chunks - 1)
                return last

            def x_hi_(k):
                return xh[:, k, :]

            def x_lo_(k):
                return xl[:, k, :]

            def unit(ph, it, j):
                pe.wait_ge(wl_rdy, it * RAW + (ph.u0 + j + 5))
                if ph.kind == "down":
                    s, first, last = (j // 2) % 2, j % 2 == 0, j % 2 == 1
                    if first:
                        pe.wait_ge(acc_free[s], it + (ph.t0 // 2 + 2))
                    mm = gemm(j % 2, FU, lambda k: hh[:, (j % 2) * FU + k, :], lambda k: hl[:, (j % 2) * FU + k, :], s, first, last)
                else:
                    pe.wait_ge(acc_free[j % 2], it * 2 + (ph.t0 // 2 + j // 2 + 2))
                    mm = gemm(j % 2, KC, x_hi_, x_lo_, j % 2, True, True)
                mm.then_inc(mm_done, 1)

            def all_read(ph):
                for s in range(2):
                    pe.wait_ge(acc_free[s], (ph.t0 + ph.tiles) // 2 + 2)

            def norm(n, ph):
                all_read(ph)
                for h in range(2):
                    for c in range(KC):
                        mm = pe.matmul(bank[4 + h][:, 0:HALF], ones[:], z[:, c, halves[h]], start=c == 0, stop=c == KC - 1)
                    mm.then_inc(ln_mean, 1)
                for h in range(2):
                    pe.wait_ge(ln_sq, 2 * n + h + 1)
                    for c in range(KC):
                        mm = pe.matmul(bank[6 + h][:, 0:HALF], ones[:], sq[:, c, halves[h]], start=c == 0, stop=c == KC - 1)
                    mm.then_inc(ln_var, 1)

            def tokens_major(R, b):
                for c in range(NBLK):
                    pe.transpose(bank[4 + b][:, c * P:(c + 1) * P], R["st"][b][:, c * P:(c + 1) * P], ident[:])
                pe.transpose(bank[6 + b][0:SAMPLE, 0:P], R["st"][b][:, SEQ:TOK], ident[:]).then_inc(tr_done, 1)

            def qkv_run(ph):
                r = ph.run
                pe.wait_ge(qs_zero, 1 + r.layer)
                with pe.Fori(0, ph.units // RAW) as it:
                    for j in range(RAW):
                        unit(ph, it, j)
                        pe.wait_ge(acc_free[(j - 1) % 2], it * 2 + ((ph.t0 + j - 1) // 2 + 3))
                        pe.wait_ge(tr_free[(j - 1) % 2], it * 2 + ((r.tr0 + j - 1) // 2 + 2))
                        tokens_major(r.R, (j - 1) % 2)
                v = ph.units - 1
                pe.wait_ge(acc_free[v % 2], (ph.t0 + v) // 2 + 3)
                pe.wait_ge(tr_free[v % 2], (r.tr0 + v) // 2 + 2)
                tokens_major(r.R, v % 2)

            def attention(ps, run):
                R = ps.R
                all_read(run.ph)
                pe.wait_ge(qk_cp, run.cp_total)
                for b in range(2):
                    pe.wait_ge(tr_free[b], (run.tr0 + run.n) // 2 + 2)

                def scores(i, blk):
                    b = blk % 2
                    pe.wait_ge(qs_rdy, i * 4 + (ps.u0 + blk + 1))
                    pe.wait_ge(sm_done, i * 4 + (ps.u0 + blk + 1))
                    for hd in range(2):
                        if ps.dilated:
                            for g in range(2):
                                rhs = R["k"][g][:, bass.ds(i, 1), blk * P:(blk + 1) * P].rearrange("p o n -> p (o n)")
                                c = hd * 256 + g * P
                                mm = pe.matmul(bank[b][:, c:c + P], R["qs"][b][:, 2 * g + hd, :], rhs, start=True, stop=True)
                        else:
                            c0 = first_col(ps, blk)
                            kt_ = i // 4 if ps is pass_a else i
                            rhs = R["k"][0][:, bass.ds(kt_, 1), (blk - 1) * P + c0:(blk + 1) * P].rearrange("p o n -> p (o n)")
                            mm = pe.matmul(bank[b][:, hd * 256 + c0:(hd + 1) * 256], R["qs"][b][:, hd, :], rhs, start=True, stop=True)
                    mm.then_inc(sc_done, 1)

                def turn(i, blk):
                    b = blk % 2
                    pe.wait_ge(ex_done, i * 4 + (ps.u0 + blk + 1))
                    pe.wait_ge(ptc_done, i * 4 + (ps.u0 + blk + 1))
                    for hd in range(2):
                        for kb in range(first_col(ps, blk) // P, 2):
                            c = hd * 256 + kb * P
                            mm = pe.transpose(bank[4 + b][:, c:c + P], R["st"][b][:, c:c + P], ident[:])
                    mm.then_inc(pt_done, 1)

                def values(i, blk):
                    b = blk % 2
                    pe.wait_ge(ptc_done, i * 4 + (ps.u0 + blk + 3))
                    pe.wait_ge(oev_done, i * 4 + (ps.u0 + blk + 1))
                    vt = i // 4 if ps is pass_a else i
                    for hd in range(2):
                        kbs = range(first_col(ps, blk) // P, 2)
                        for kb in kbs:
                            if ps.dilated:
                                src = R["v"][kb][:, blk, bass.ds(vt * P, P)]
                            else:
                                src = R["v"][0][:, blk - 1 + kb, bass.ds(vt * P, P)]
                            c = hd * 256 + kb * P
                            mm = pe.matmul(bank[2 + b][:, hd * P:(hd + 1) * P], R["kt"][b][:, c:c + P], src,
                                           start=kb == kbs[0], stop=kb == kbs[-1])
                    mm.then_inc(pv_done, 1)
                skewed(pe, ps.pairs, [(scores, 0), (turn, 1), (values, 2)])
                end = ps.u0 + ps.units
                pe.wait_ge(sm_done, end + 2)
                pe.wait_ge(ptc_done, end + 2)
                pe.wait_ge(oev_done, end + 2)

            def outputs_a():
                for b in range(NBLK):
                    pe.wait_ge(ow_rdy, b + 1)
                for p_ in range(PAIRS):
                    if p_ >= 2:
                        pe.wait_ge(ot_v, p_ - 1)
                    for b in range(NBLK):
                        mm = pe.transpose(bank[6 + p_ % 2][:, b * P:(b + 1) * P], RA["o"][0][:, b, p_ * P:(p_ + 1) * P], ident[:])
                    mm.then_inc(ot_done, 1)

            def outputs_b(r):
                pe.wait_ge(ow_rdy, NBLK + 8 * (r + 1))
                for p_ in range(4):
                    if p_:
                        pe.wait_ge(ot_v, PAIRS + 4 * r + p_)
                    for y in range(2):
                        for b in range(NBLK):
                            mm = pe.transpose(bank[6 + y][:, b * P:(b + 1) * P], RB["o"][y][:, b, p_ * P:(p_ + 1) * P], ident[:])
                    mm.then_inc(ot_done, 1)

            def decode(layer):
                L = LAYER[layer]
                D, G, kv = L["D"], L["G"], L["kv"]
                if layer == 0:
                    pe.wait_ge(ot_v, PAIRS)
                else:
                    pe.wait_ge(ot_v, PAIRS + 8)
                pe.wait_ge(d_q2, 2 * (layer + 1))
                for y in L["prod"]:
                    if y.k >= 2:
                        pe.wait_ge(d_qb, y.k - 1)
                    tok = y.n * DEC + y.tau
                    for c in range(2):
                        mm = pe.matmul(bank[2 * (y.k % 2) + c][:], pick[:, tok:tok + 1].to_broadcast([P, P]),
                                       D["q2"][:, y.g, c * 512:(c + 1) * 512], start=True, stop=True)
                    mm.then_inc(d_qp, 1)
                pe.wait_ge(d_red, L["prod"][-1].k + 1)
                for T in range(4):
                    k = 4 * layer + T
                    if T >= 2:
                        pe.wait_ge(d_sv, k - 1)
                    for g in range(G):
                        mm = pe.transpose(bank[4 + T % 2][:, g * P:(g + 1) * P], D["s"][:, g, T * P:(T + 1) * P], ident[:])
                    mm.then_inc(d_st, 1)
                for T in range(4):
                    k = 4 * layer + T
                    pe.wait_ge(d_nm, 3 * k + 3)
                    if T >= 2:
                        pe.wait_ge(d_ptc, k - 1)
                    for g in range(G):
                        mm = pe.transpose(bank[6 + T % 2][:, g * P:(g + 1) * P], D["sm"][T % 2][:, g * P:(g + 1) * P], ident[:])
                    mm.then_inc(d_pt, 1)
                pe.wait_ge(d_ptc, 4 * layer + 4)
                nb = (kv * HD) // 256 // 2 or 1
                w = kv * HD // nb
                for x in L["v"]:
                    n, g, taus = x.what
                    if g == 0 and n >= 2:
                        pe.wait_ge(d_msk, NS * layer + n - 1)
                    pe.wait_ge(d_kv[x.slot], x.val)
                    for tau in taus:
                        for c in range(nb):
                            mm = pe.matmul(bank[2 * (n % 2) + c][32 * tau:32 * tau + 32, 0:w], D["p"][:, g, n * DEC + tau, :],
                                           D["kv"][x.slot][:, c * w:(c + 1) * w], start=g == 0, stop=g == G - 1,
                                           tile_position=(0, 32 * tau), skip_group_check=True)
                    mm.then_inc(d_pv, 1)
                pe.wait_ge(d_sum, layer + 1)
                for p_ in range(PAIRS):
                    src = D["qn"][0:SAMPLE, 0, :] if layer == 0 else D["ot"][:]
                    mm = pe.transpose(bank[4][:, p_ * SAMPLE:(p_ + 1) * SAMPLE], src[:, p_ * P:(p_ + 1) * P], ident[0:SAMPLE, 0:SAMPLE])
                mm.then_inc(d_tt, 1)
                pe.wait_ge(d_tv, layer + 1)

            pe.wait_ge(cst_ld, 16 * (5 + 6 * DEPTH))
            pe.wait_ge(setup, 2)
            pe.matmul(bank[0][0:HEADS, :], tab[:], oh1[:, 0:512], start=True, stop=True)
            pe.matmul(bank[1][0:HEADS, 0:LINES - 512], tab[:], oh1[:, 512:LINES], start=True, stop=True)
            pe.matmul(bank[2][0:HEADS, 0:ND], tab[:], oh2[:], start=True, stop=True).then_inc(line_t, 1)
            pe.wait_ge(in_ld, 32)
            pe.wait_ge(line_c, 1)
            for c in range(KC):
                if c >= 4:
                    pe.wait_ge(ln_aff, c - 3)
                for b in range(NBLK):
                    pe.transpose(bank[c % 4][:, b * P:(b + 1) * P], xin[:, b, c * P:(c + 1) * P], ident[:])
                pe.transpose(bank[4 + c % 4][:, 0:SAMPLE], xsin[:, c * P:(c + 1) * P], ident[0:SAMPLE, 0:SAMPLE]).then_inc(init_t, 1)

            n_norm = 0
            ffn = 0
            for ph in phases:
                if ph.kind == "up":
                    pe.wait_ge(x_lo, KC * (n_norm + 1))
                    with pe.Fori(0, ph.units // RAW) as it:
                        for j in range(RAW):
                            unit(ph, it, j)
                elif ph.kind == "down":
                    ffn += 1
                    pe.wait_ge(hl_rdy, FC * ffn + 2)
                    with pe.Fori(0, ph.units // RAW) as it:
                        for j in range(RAW):
                            unit(ph, it, j)
                    norm(n_norm, ph)
                    n_norm += 1
                elif ph.kind == "qkv":
                    pe.wait_ge(x_lo, KC * (n_norm + 1))
                    qkv_run(ph)
                    if ph is qkv[0]:
                        attention(pass_a, ph.run)
                        outputs_a()
                        decode(0)
                    else:
                        r, y = ph.run.rnd, int(ph.run.items[0][1] > 0)
                        attention(pass_b[2 * r + y], ph.run)
                        if y:
                            outputs_b(r)
                            if r:
                                pe.wait_ge(sp_l, 2)
                                decode(1)
                            else:
                                pe.wait_ge(ot_v, PAIRS + 4)
                else:
                    with pe.Fori(0, ph.units // RAW) as it:
                        for j in range(RAW):
                            unit(ph, it, j)
                    norm(n_norm, ph)
                    n_norm += 1
            pe.wait_ge(ln_aff, KC * (3 * DEPTH + 1))
            for b in range(NBLK + 1):
                if b >= 2:
                    pe.wait_ge(out_ca, b - 1)
                    pe.wait_ge(out_cv, b - 1)
                w = P if b < NBLK else SAMPLE
                for c in range(KC):
                    mm = pe.transpose(bank[2 * (b % 2) + c // 4][0:w, (c % 4) * P:(c % 4 + 1) * P], z[:, c, b * P:b * P + w], ident[:])
                mm.then_inc(out_t, 1)

        def units_ahead(eng, ph, split, read):
            n = ph.units // RAW
            with eng.Fori(0, n - 1) as it:
                for j in range(RAW):
                    split(ph, it * RAW + (j + 1), (j + 1) % RAW, it + (j + 1) // RAW)
                    read(ph, it, j)
            for j in range(RAW):
                if j < RAW - 1:
                    split(ph, RAW * (n - 1) + j + 1, j + 1, n - 1)
                elif ph.next:
                    split(ph.next, 0, 0, 0)
                read(ph, n - 1, j)

        def stage_tile(eng, copy, r, i):
            st, s, g = r.R["st"][i % 2], i % 2, r.items[i][1]
            eng.wait_ge(mm_done, r.ph.u0 + i + 3)
            if r.td0 + i > 0:
                eng.wait_ge(tr_done, r.td0 + i)
            if i >= 2 and r.items[i - 2][2] != "v":
                eng.wait_ge(qk_cp, r.cp_after[i - 2])
            if g == 0:
                copy(st[:, halves[0]], acc(s, 0))
                copy(st[:, halves[1]], acc(s, 1)).then_inc(acc_free[s], 1)
            else:
                u0, u1 = HALF // 4, (SEQ - HALF) // 4
                v = st[:, 0:SEQ].rearrange("p (c u) -> p c u", c=4)
                copy(v[:, :, 0:u0], acc(s, 0).rearrange("p (u c) -> p c u", c=4))
                copy(v[:, :, u0:u0 + u1], acc(s, 1)[:, 0:SEQ - HALF].rearrange("p (u c) -> p c u", c=4))
                copy(st[:, SEQ:TOK], acc(s, 1)[:, SEQ - HALF:HALF]).then_inc(acc_free[s], 1)

        def keep_tokens(eng, copy, r, i):
            b, (gi, g, kind, p_) = i % 2, r.items[i]
            eng.wait_ge(tr_done, r.td0 + i + 2)
            if kind == "k":
                if r.kt_before[i]:
                    eng.wait_ge(kt_out[b], r.kt_before[i])
                copy(r.R["kt"][b][:], bank[4 + b][:])
            if kind == "v":
                if r.v_total > 16 * 4:
                    eng.wait_ge(v_out, r.v_before)
                copy(r.R["v"][gi][:, :, p_ * P:(p_ + 1) * P], bank[4 + b][:].rearrange("p (c n) -> p c n", c=NBLK))
            if r.ss_before[i]:
                eng.wait_ge(ss_out[b], r.ss_before[i])
            copy(r.R["ss"][b][:], bank[6 + b][0:SAMPLE, 0:P]).then_inc(tr_free[b], 1)
        for n_, r in enumerate(runs):
            r.v_before = runs[n_ - 1].v_total if n_ else 0

        @block.scalar
        def _(act):
            def split(ph, i, j, it):
                act.wait_ge(raw_in[j], it * (16 * ph.dmas) + (ph.land0[j] + 16 * ph.dmas))
                act.wait_ge(mm_done, i + (ph.u0 + 1))
                act.copy(wh[j % 2][:, 0:ph.chunks, :], raw[j][:, 0:ph.chunks, :]).then_inc(wh_rdy, 1)

            def read(ph, it, j):
                if ph.kind == "up" and j % 2 == 0:
                    b = j // 2
                    act.wait_ge(mm_done, it * RAW + (ph.u0 + j + 3))
                    act.wait_ge(acc_free[1], it * 2 + (ph.t0 // 2 + b + 1))
                    act.activation(sil[b][:, halves[0]], acc(0, 0), ACT.Silu)
                    act.activation(sil[b][:, halves[1]], acc(0, 1), ACT.Silu).then_inc(acc_free[0], 1)

            def norm(n, last):
                for h in range(2):
                    act.wait_ge(ln_dev, 2 * n + h + 1)
                    act.activation(sq[:, :, halves[h]], z[:, :, halves[h]], ACT.Square).then_inc(ln_sq, 1)
                for h in range(2):
                    act.wait_ge(ln_rs, 2 * (2 * n + h) + 2)
                    act.activation(rstd[:, halves[h]], rstd[:, halves[h]], ACT.Sqrt).then_inc(ln_root, 1)
                act.wait_ge(ln_nrm, 2 * n + 2)
                for c in range(KC):
                    act.activation(z[:, c, :], z[:, c, :], ACT.Identity, bias=shift[:, n, c:c + 1],
                                   scale=gain[:, n, c:c + 1]).then_inc(ln_aff, 1)
                if not last:
                    high(n + 1)

            def high(k):
                for c in range(KC):
                    act.wait_ge(ln_aff, KC * k + c + 1)
                    act.copy(xh[:, c, :], z[:, c, :]).then_inc(x_hi, 1)

            def stage(r, i):
                stage_tile(act, act.copy, r, i)

            def run(ph):
                r = ph.run
                for i in range(r.n):
                    if i + 1 < r.n:
                        split(ph, i + 1, (i + 1) % RAW, (i + 1) // RAW)
                    else:
                        split(ph.next, 0, 0, 0)
                    if i % 2 == 0:
                        stage(r, i)
                    elif i:
                        pass
                    if i >= 1 and (i - 1) % 2 == 1:
                        keep_tokens(act, act.copy, r, i - 1)
                keep_tokens(act, act.copy, r, r.n - 1)

            def attention(ps, rn):
                R = ps.R
                for b in range(2):
                    act.wait_ge(kt_out[b], rn.kt_total[b])

                def exps(i, blk):
                    b, c0 = blk % 2, first_col(ps, blk)
                    act.wait_ge(nm_done, i * 4 + (ps.u0 + blk + 1))
                    for hd in range(2):
                        x = R["st"][b][:, hd * 256 + c0:(hd + 1) * 256]
                        last = act.activation(x, x, ACT.Exp, bias=R["nm"][b][:, hd:hd + 1], accum_out=R["dn"][b][:, hd:hd + 1])
                    last.then_inc(ex_done, 1)

                def copy(i, blk):
                    b, c0 = blk % 2, first_col(ps, blk)
                    act.wait_ge(pt_done, i * 4 + (ps.u0 + blk + 3))
                    act.wait_ge(pv_done, i * 4 + (ps.u0 + blk + 1))
                    v = R["kt"][b][:].rearrange("p (h k) -> p h k", h=2)[:, :, c0:256]
                    act.copy(v, bank[4 + b][:].rearrange("p (h k) -> p h k", h=2)[:, :, c0:256]).then_inc(ptc_done, 1)
                skewed(act, ps.pairs, [(exps, 0), (copy, 1)])

            def weights(k):
                R, y = (RA, 0) if k == 0 else (RB, (k - 1) % 2)
                act.wait_ge(cmb_v, 7 * k + 3)
                act.activation(R["t"][1][:], R["t"][1][:], ACT.Exp)
                act.activation(R["t"][2][:], R["t"][2][:], ACT.Exp).then_inc(cmb_a, 1)

            def outputs_a():
                for p_ in range(PAIRS):
                    act.wait_ge(ot_done, p_ + 1)
                    act.copy(xh[:, p_, 0:SEQ], bank[6 + p_ % 2][:]).then_inc(ot_a, 1)

            def keep_high(r):
                act.wait_ge(ot_v, PAIRS + 4 * (r + 1))
                act.copy(xh[:, 4 * r:4 * r + 4, 0:SEQ], RB["at"][:]).then_inc(sp_h, 1)

            def outputs_b(r):
                if r:
                    keep_high(0)
                    act.wait_ge(sp_l, 1)
                for p_ in range(4):
                    act.wait_ge(ot_done, PAIRS + 4 * r + p_ + 1)
                    if p_ >= 2:
                        act.wait_ge(ot_v, PAIRS + 4 * r + p_ - 1)
                    act.copy(RB["st"][p_ % 2][:, 0:SEQ], bank[6][:]).then_inc(ot_a, 1)
                if r:
                    keep_high(1)

            def decode(layer):
                L = LAYER[layer]
                D, G, kv, new = L["D"], L["G"], L["kv"], L["new"]
                act.wait_ge(d_qn, 32 * (layer + 1))
                act.wait_ge(d_zero, 2 * layer + 1)
                act.copy(D["q2"][0:2 * SAMPLE], D["qn"][:]).then_inc(d_q2, 1)
                for m, y in enumerate(L["prod"]):
                    act.wait_ge(d_qp, y.k + 1)
                    if m >= 3:
                        act.wait_ge(*L["prod"][m - 3].mult)
                    for c in range(2):
                        last = act.copy(D["qb"][y.slot][:, c * 512:(c + 1) * 512], bank[2 * (y.k % 2) + c][:])
                    last.then_inc(d_qb, 1)
                    if m == len(L["prod"]) * 3 // 4:
                        new_scores(layer)
                act.wait_ge(d_sn_out, 16 * (layer + 1))
                act.dma_start(D["snb"][:], snew_d[layer].rearrange("(t p) c -> p t c", p=P)).then_inc(d_sn_in, 16)
                W = G * P + new + (1 if layer == 0 else 0)
                for T in range(4):
                    k = 4 * layer + T
                    act.wait_ge(d_nm, 3 * k + 1)
                    act.activation(D["sm"][T % 2][:, 0:W], D["sm"][T % 2][:, 0:W], ACT.Exp, bias=D["st"][:, T, 0:1],
                                   accum_out=D["st"][:, T, 1:2]).then_inc(d_ex, 1)
                    if T:
                        cached_probs(layer, T - 1)
                cached_probs(layer, 3)
                act.wait_ge(d_nm, 3 * (4 * layer + 3) + 3)
                act.dma_start(pnew_d[layer].rearrange("(t p) c -> p t c", p=P), D["pnb"][:]).then_inc(d_pn_out, 16)
                act.wait_ge(d_pn_out, 16 * (layer + 1))
                act.dma_start(D["pn"][:].rearrange("s h c -> s (h c)"), pnew_d[layer].rearrange("(s h) c -> s (h c)", h=HEADS)).then_inc(d_pn_in, 16)
                act.wait_ge(d_oc, NS * (layer + 1))
                for tau in range(DEC):
                    dst = odec_d[layer].rearrange("(n t) (h d) -> t h n d", t=DEC, d=HD)[tau]
                    act.dma_start(dst, D["oc"][32 * tau:32 * tau + HEADS, :, :]).then_inc(d_oc_out, 16)
                act.wait_ge(d_oc_out, 16 * DEC * (layer + 1))
                act.dma_start(D["ot"][:], odec_d[layer]).then_inc(d_ot_in, 16)
                act.wait_ge(d_tt, layer + 1)
                act.copy(xh[:, :, SEQ:TOK], bank[4][:, 0:KC * SAMPLE].rearrange("p (c s) -> p c s", c=KC)).then_inc(d_ta, 1)

            def new_scores(layer):
                L = LAYER[layer]
                act.wait_ge(d_nv, L["kn"][-1].done[0][1])
                act.dma_start(snew_d[layer].rearrange("(s h) c -> s (h c)", h=HEADS), L["D"]["snew"][:].rearrange("s h c -> s (h c)")).then_inc(d_sn_out, 16)

            def cached_probs(layer, T):
                D, G = LAYER[layer]["D"], LAYER[layer]["G"]
                act.wait_ge(d_pt, 4 * layer + T + 1)
                for g in range(G):
                    v = bank[6 + T % 2][:, g * P:(g + 1) * P].rearrange("p (s h) -> p s h", h=HEADS)
                    last = act.copy(D["p"][:, g, 8 * T:8 * T + 8, 0:HEADS], v)
                last.then_inc(d_ptc, 1)

            act.wait_ge(cst_ld, 16 * (5 + 6 * DEPTH))
            act.copy(pick[:], pick32[:])
            act.wait_ge(line_c, 2)
            for l, c0 in enumerate((0, LINE_X, LINE_X + LINE_Y)):
                W = lines_d[l].shape[2]
                act.dma_start(lines_d[l], lin1[:, None, c0:c0 + W].to_broadcast([HEADS, P, W])).then_inc(line_o, 16)
            act.dma_start(dec_lines_d, lin2[:]).then_inc(line_o, 16)
            for c in range(KC):
                act.wait_ge(init_t, c + 1)
                act.copy(z[:, c, 0:SEQ], bank[c % 4][:])
                act.copy(z[:, c, SEQ:TOK], bank[4 + c % 4][:, 0:SAMPLE]).then_inc(ln_aff, 1)
            high(0)
            split(phases[0], 0, 0, 0)
            act.wait_ge(line_o, 64)
            n_norm = 0
            for ph in phases:
                if ph.kind == "qkv":
                    run(ph)
                    if ph is qkv[0]:
                        attention(pass_a, ph.run)
                        weights(0)
                        outputs_a()
                        decode(0)
                    else:
                        r, y = ph.run.rnd, int(ph.run.items[0][1] > 0)
                        attention(pass_b[2 * r + y], ph.run)
                        if y:
                            weights(1 + 2 * r)
                            weights(2 + 2 * r)
                            outputs_b(r)
                            if r:
                                decode(1)
                else:
                    units_ahead(act, ph, split, read)
                    if ph.kind != "up":
                        norm(n_norm, ph.next is None)
                        n_norm += 1
            for b in range(NBLK + 1):
                w = P if b < NBLK else SAMPLE
                act.wait_ge(out_t, b + 1)
                act.copy(yout[0:w, b, 0:512], bank[2 * (b % 2)][0:w, :]).then_inc(out_ca, 1)
            act.wait_ge(out_ca, NBLK + 1)
            act.wait_ge(out_cv, NBLK + 1)
            act.dma_start(o["y_prompt"][0].rearrange("(b p) d -> p b d", p=P), yout[:, 0:NBLK, :]).then_inc(out_done, 16)
            act.dma_start(o["y_sample"].rearrange("n t d -> (n t) d"), yout[0:SAMPLE, NBLK, :]).then_inc(out_done, 16)

        @block.vector
        def _(dve):
            steps = {"cmb": 0}

            def split(ph, i, j, it):
                dve.wait_ge(wh_rdy, i + (ph.u0 + 1))
                v = wh[j % 2][:, 0:ph.chunks, :]
                dve.tensor_tensor(wl[j % 2][:, 0:ph.chunks, :], raw[j][:, 0:ph.chunks, :], v.bitcast(F32), ALU.subtract).then_inc(wl_rdy, 1)

            def read(ph, it, j):
                if ph.kind == "up" and j % 2 == 1:
                    b = j // 2
                    dve.wait_ge(mm_done, it * RAW + (ph.u0 + j + 3))
                    dve.wait_ge(acc_free[0], it * 2 + (ph.t0 // 2 + b + 3))
                    dve.wait_ge(hl_rdy, it * 2 + (FC * ph.ffn + b + 1))
                    for h in range(2):
                        last = dve.tensor_tensor(h32[b][:, halves[h]], sil[b][:, halves[h]], acc(1, h), ALU.mult)
                    last.then_inc(acc_free[1], 1)
                elif ph.kind == "down" and j % 2 == 1:
                    add_tile(ph, it * RAW + (ph.u0 + j + 3), it * 2 + j // 2, j // 2, 0.5)
                elif ph.kind == "wo":
                    add_tile(ph, it * RAW + (ph.u0 + j + 3), it * RAW + j, j % 2, 1.0)

            def add_tile(ph, done, chunk, s, factor):
                dve.wait_ge(mm_done, done)
                for h in range(2):
                    v = z[:, bass.ds(chunk, 1), halves[h]].rearrange("p o n -> p (o n)")
                    last = dve.scalar_tensor_tensor(v, acc(s, h), factor, v, ALU.mult, ALU.add)
                last.then_inc(acc_free[s], 1)

            def norm(n, last):
                for h in range(2):
                    v = z[:, :, halves[h]]
                    dve.wait_ge(ln_mean, 2 * n + h + 1)
                    m = bank[4 + h][:, None, 0:HALF].to_broadcast([P, KC, HALF])
                    dve.tensor_tensor(v, v, m, ALU.subtract).then_inc(ln_dev, 1)
                for h in range(2):
                    dve.wait_ge(ln_var, 2 * n + h + 1)
                    dve.tensor_scalar(rstd[:, halves[h]], bank[6 + h][:, 0:HALF], LN_EPS, None, ALU.add).then_inc(ln_rs, 1)
                    dve.wait_ge(ln_rs, 2 * (2 * n + h) + 1)
                    dve.reciprocal(rstd[:, halves[h]], rstd[:, halves[h]]).then_inc(ln_rs, 1)
                    dve.wait_ge(ln_root, 2 * n + h + 1)
                    v = z[:, :, halves[h]]
                    dve.tensor_tensor(v, v, rstd[:, None, halves[h]].to_broadcast([P, KC, HALF]), ALU.mult).then_inc(ln_nrm, 1)
                if not last:
                    low(n + 1)

            def low(k):
                for c in range(KC):
                    dve.wait_ge(x_hi, KC * k + c + 1)
                    dve.tensor_tensor(xl[:, c, :], z[:, c, :], xh[:, c, :].bitcast(F32), ALU.subtract).then_inc(x_lo, 1)

            def run(ph):
                r = ph.run
                for i in range(r.n):
                    if i + 1 < r.n:
                        split(ph, i + 1, (i + 1) % RAW, (i + 1) // RAW)
                    else:
                        split(ph.next, 0, 0, 0)
                    if i % 2 == 1:
                        stage_tile(dve, dve.tensor_copy, r, i)
                    if i >= 1 and (i - 1) % 2 == 0:
                        keep_tokens(dve, dve.tensor_copy, r, i - 1)

            def attention(ps, rn):
                R = ps.R
                dve.wait_ge(bias_ld, BIAS_LD[ps.n])

                def add_bias(i, blk):
                    b, c0 = blk % 2, first_col(ps, blk)
                    dve.wait_ge(sc_done, i * 4 + (ps.u0 + blk + 3))
                    dve.wait_ge(pt_done, i * 4 + (ps.u0 + blk + 1))
                    x = R["st"][b][:, 0:SEQ].rearrange("p (h k) -> p h k", h=2)[:, :, c0:256]
                    s = bank[b][:].rearrange("p (h k) -> p h k", h=2)[:, :, c0:256]
                    dve.scalar_tensor_tensor(x, s, SCALE, R["bias"][:, bass.ds(i * 2, 2), c0:256], ALU.mult, ALU.add).then_inc(sm_done, 1)
                    dve.wait_ge(sm_done, i * 4 + (ps.u0 + blk + 3))
                    dve.tensor_reduce(R["nm"][b][:], x, AX_X, ALU.max, negate=True).then_inc(nm_done, 1)

                def output(i, blk):
                    b = blk % 2
                    dve.wait_ge(pv_done, i * 4 + (ps.u0 + blk + 3))
                    o_ = R["o"][ps.slot][:, blk, bass.ds(i * P, P)].rearrange("p (h d) -> p h d", h=2)
                    dve.tensor_copy(o_, bank[2 + b][:, 0:256].rearrange("p (a d) -> p a d", d=HD)[:, 0:4:3, :]).then_inc(oev_done, 1)

                def stats(i, blk):
                    b = blk % 2
                    dve.wait_ge(ex_done, i * 4 + (ps.u0 + blk + 1))
                    md = R["md"][ps.slot]
                    dve.tensor_copy(md[:, blk, 0, bass.ds(i * 2, 2)], R["nm"][b][:])
                    dve.tensor_copy(md[:, blk, 1, bass.ds(i * 2, 2)], R["dn"][b][:]).then_inc(st_done, 1)
                skewed(dve, ps.pairs, [(add_bias, 0), (stats, 1), (output, 3)])

            def step(ins):
                steps["cmb"] += 1
                ins.then_inc(cmb_v, 1)
                dve.wait_ge(cmb_v, steps["cmb"])

            def weights(k):
                R, y = (RA, 0) if k == 0 else (RB, (k - 1) % 2)
                own, oth, tt = R["md"][y], R["mo"][y], R["t"]
                if k:
                    dve.wait_ge(md_in, 16 * (2 * ((k - 1) // 2) + 2))
                step(dve.tensor_tensor(tt[0][:], own[:, :, 0, :], oth[:, :, 0, :], ALU.min))
                step(dve.tensor_tensor(tt[1][:], tt[0][:], own[:, :, 0, :], ALU.subtract))
                step(dve.tensor_tensor(tt[2][:], tt[0][:], oth[:, :, 0, :], ALU.subtract))
                dve.wait_ge(cmb_a, k + 1)
                step(dve.tensor_tensor(tt[3][:], tt[1][:], own[:, :, 1, :], ALU.mult))
                step(dve.tensor_tensor(tt[4][:], tt[2][:], oth[:, :, 1, :], ALU.mult))
                step(dve.tensor_tensor(tt[3][:], tt[3][:], tt[4][:], ALU.add))
                dve.reciprocal(tt[3][:], tt[3][:]).then_inc(cmb_r, 1)
                dve.wait_ge(cmb_r, k + 1)
                step(dve.tensor_tensor(tt[1][:], tt[1][:], tt[3][:], ALU.mult))
                n = HEADS if k == 0 else PAIRS
                for b in range(NBLK):
                    v = R["o"][y][:, b, :].rearrange("p (h d) -> p h d", d=HD)
                    dve.tensor_tensor(v, v, tt[1][:, b, :, None].to_broadcast([P, n, HD]), ALU.mult).then_inc(ow_rdy, 1)

            def outputs_a():
                for p_ in range(PAIRS):
                    dve.wait_ge(ot_a, p_ + 1)
                    dve.tensor_tensor(xl[:, p_, 0:SEQ], bank[6 + p_ % 2][:], xh[:, p_, 0:SEQ].bitcast(F32), ALU.subtract).then_inc(ot_v, 1)

            def keep_low(r):
                dve.wait_ge(sp_h, r + 1)
                dve.tensor_tensor(xl[:, 4 * r:4 * r + 4, 0:SEQ], RB["at"][:], xh[:, 4 * r:4 * r + 4, 0:SEQ].bitcast(F32), ALU.subtract).then_inc(sp_l, 1)

            def outputs_b(r):
                if r:
                    keep_low(0)
                    dve.wait_ge(sp_l, 1)
                for p_ in range(4):
                    dve.wait_ge(ot_a, PAIRS + 4 * r + p_ + 1)
                    v = RB["at"][:, p_, :].rearrange("p (u c) -> p u c", c=4)
                    y = bank[7][:].rearrange("p (c u) -> p u c", c=4)
                    x = RB["st"][p_ % 2][:, 0:SEQ].rearrange("p (u c) -> p u c", c=4)
                    dve.tensor_tensor(v, y, x, ALU.add).then_inc(ot_v, 1)
                if r:
                    keep_low(1)

            def decode(layer):
                L = LAYER[layer]
                D, G, kv, new = L["D"], L["G"], L["kv"], L["new"]
                rep = HEADS // kv
                dve.wait_ge(d_q2, 2 * layer + 1)
                low_rows = slice(SAMPLE, 2 * SAMPLE)
                dve.tensor_tensor(D["q2"][low_rows], D["qn"][low_rows], D["q2"][low_rows].bitcast(F32), ALU.subtract).then_inc(d_q2, 1)
                nv = [L["nv0"]]

                def nstep(ins):
                    nv[0] += 1
                    ins.then_inc(d_nv, 1)

                def heads_of(ap):
                    v = ap.rearrange("p (k d) -> p k d", d=HD)
                    return v[:, :, None, :].to_broadcast([ap.shape[0], kv, rep, HD])

                def by_head(ap):
                    return ap.rearrange("p (k r d) -> p k r d", r=rep, d=HD)

                def new_key(x):
                    c_, g, tp = x.what
                    dve.wait_ge(d_kn[x.slot], x.landed)
                    nstep(dve.tensor_tensor(by_head(D["ot"][:]), heads_of(D["kn"][x.slot][:]), by_head(D["qn"][0:SAMPLE, g, :]), ALU.mult))
                    dve.wait_ge(d_nv, nv[0])
                    nstep(dve.tensor_reduce(D["snew"][:, :, c_:c_ + 1].rearrange("s h c -> s (h c)"), D["ot"][:].rearrange("s (h d) -> s h d", d=HD), AX_X, ALU.add))
                    dve.wait_ge(d_nv, nv[0])

                def product(y):
                    dve.wait_ge(d_kv[y.tile.slot], y.tile.val)
                    dve.wait_ge(d_qb, y.k + 1)
                    if y.k >= 3:
                        dve.wait_ge(d_red, y.k - 2)
                    dve.tensor_tensor(by_head(D["pr"][y.slot][:]), heads_of(D["kv"][y.tile.slot][:]), by_head(D["qb"][y.slot][:]), ALU.mult).then_inc(d_mult[1], 1)

                for m, x in enumerate(L["k"]):
                    for y in x.prods:
                        if y.by:
                            product(y)
                        dve.wait_ge(*y.mult)
                        tok = y.n * DEC + y.tau
                        dve.tensor_reduce(D["s"][:, y.g, tok * HEADS:(tok + 1) * HEADS], D["pr"][y.slot][:].rearrange("p (h d) -> p h d", d=HD),
                                          AX_X, ALU.add).then_inc(d_red, 1)
                    if m < len(L["kn"]):
                        new_key(L["kn"][m])
                dve.wait_ge(d_cst, 16 * (cst_dmas[0] + (cst_dmas[1] if layer else 0)))
                dve.wait_ge(d_sn_in, 16 * (layer + 1))
                W = G * P + new + (1 if layer == 0 else 0)

                def shift_max(T):
                    k, sm = 4 * layer + T, D["sm"][T % 2]
                    dve.wait_ge(d_st, k + 1)
                    if T >= 2:
                        dve.wait_ge(d_pt, k - 1)
                    dve.scalar_tensor_tensor(sm[:, 0:G * P], bank[4 + T % 2][:, 0:G * P], SCALE, D["bc"][:].rearrange("p g r -> p (g r)"),
                                             ALU.mult, ALU.add).then_inc(d_sv, 1)
                    dve.scalar_tensor_tensor(sm[:, G * P:G * P + new], D["snb"][:, T, :], SCALE, D["bn"][:], ALU.mult, ALU.add).then_inc(d_sx, 1)
                    if layer == 0:
                        dve.tensor_copy(sm[:, W - 1:W], D["snk"][:]).then_inc(d_sx, 1)
                        dve.wait_ge(d_sx, 2 * k + 2)
                    else:
                        dve.wait_ge(d_sx, 8 + T + 1)
                    dve.wait_ge(d_sv, k + 1)
                    dve.tensor_reduce(D["st"][:, T, 0:1], sm[:, 0:W], AX_X, ALU.max, negate=True).then_inc(d_nm, 1)

                def normalise(T):
                    k, sm = 4 * layer + T, D["sm"][T % 2]
                    dve.wait_ge(d_ex, k + 1)
                    dve.reciprocal(D["st"][:, T, 2:3], D["st"][:, T, 1:2]).then_inc(d_nm, 1)
                    dve.wait_ge(d_nm, 3 * k + 2)
                    dve.tensor_scalar(D["pnb"][:, T, :], sm[:, G * P:G * P + new], D["st"][:, T, 2:3], None, ALU.mult)
                    dve.tensor_scalar(sm[:, 0:G * P], sm[:, 0:G * P], D["st"][:, T, 2:3], None, ALU.mult).then_inc(d_nm, 1)
                for T in range(4):
                    shift_max(T)
                    normalise(T)
                nb = (kv * HD) // 256 // 2 or 1
                for n in range(NS):
                    for x in L["v"]:
                        if x.what[0] == n:
                            end = x.done[0][1]
                    dve.wait_ge(d_pv, end)
                    w = kv * HD // nb
                    tmp = D["pr"][n % 2]
                    for c in range(nb):
                        q = w // HD
                        m = D["mask"][:, c * q:(c + 1) * q, None].to_broadcast([P, q, HD])
                        src = bank[2 * (n % 2) + c][:, 0:w].rearrange("p (h d) -> p h d", d=HD)
                        last = dve.tensor_tensor(tmp[:, c * w:(c + 1) * w].rearrange("p (h d) -> p h d", d=HD), src, m, ALU.mult)
                    last.then_inc(d_msk, 1)
                    dve.wait_ge(d_msk, NS * layer + n + 1)
                    dve.tensor_reduce(D["oc"][:, n, :], tmp[:, 0:kv * HD].rearrange("p (h d) -> p d h", d=HD), AX_X, ALU.add).then_inc(d_oc, 1)
                dve.wait_ge(d_ot_in, 16 * (layer + 1))
                dve.wait_ge(d_pn_in, 16 * (layer + 1))
                nv[0] = L["vn"][0].done[0][1] - 2
                tmp = D["qn"][0:SAMPLE, 0, :]
                for x in L["vn"]:
                    c_, g, tp = x.what
                    dve.wait_ge(d_kn[x.slot], x.landed)
                    p_ = D["pn"][:, :, c_:c_ + 1].rearrange("s (k r) c -> s k r c", r=rep).to_broadcast([SAMPLE, kv, rep, HD])
                    nstep(dve.tensor_tensor(by_head(tmp), heads_of(D["kn"][x.slot][:]), p_, ALU.mult))
                    dve.wait_ge(d_nv, nv[0])
                    nstep(dve.tensor_tensor(D["ot"][:], D["ot"][:], tmp, ALU.add))
                    dve.wait_ge(d_nv, nv[0])
                if layer == 0:
                    dst = tmp.rearrange("s (g r h d) -> s g h r d", g=2, h=2, d=HD)
                    src = D["ot"][:].rearrange("s (g h r d) -> s g h r d", g=2, h=2, d=HD)
                    for g in range(2):
                        last = dve.tensor_copy(dst[:, g], src[:, g])
                    last.then_inc(d_sum, 1)
                else:
                    dve.sem_inc(d_sum, 1)
                dve.wait_ge(d_ta, layer + 1)
                v = bank[4][:, 0:KC * SAMPLE].rearrange("p (c s) -> p c s", c=KC)
                dve.tensor_tensor(xl[:, :, SEQ:TOK], v, xh[:, :, SEQ:TOK].bitcast(F32), ALU.subtract).then_inc(d_tv, 1)

            dve.memset(tab[NUM_BUCKETS:NUM_BUCKETS + 1, :], 1.0).then_inc(setup, 1)
            dve.wait_ge(line_t, 1)
            dve.tensor_copy(lin1[:, 0:512], bank[0][0:HEADS, :])
            dve.tensor_copy(lin1[:, 512:LINES], bank[1][0:HEADS, 0:LINES - 512])
            dve.tensor_copy(lin2[:], bank[2][0:HEADS, 0:ND]).then_inc(line_c, 2)
            low(0)
            split(phases[0], 0, 0, 0)
            dve.wait_ge(line_o, 64)
            n_norm = 0
            for ph in phases:
                if ph.kind == "qkv":
                    run(ph)
                    if ph is qkv[0]:
                        attention(pass_a, ph.run)
                        mo = RA["mo"][0]
                        for b in range(NBLK):
                            dve.tensor_scalar(mo[:, b, 0, :], RA["sink"][:], -1.0, None, ALU.mult)
                        dve.memset(mo[:, :, 1, :], 1.0).then_inc(sink_rdy, 1)
                        dve.wait_ge(sink_rdy, 1)
                        dve.wait_ge(st_done, pass_a.units)
                        dve.wait_ge(oev_done, pass_a.units + 2)
                        weights(0)
                        outputs_a()
                        decode(0)
                    else:
                        r, y = ph.run.rnd, int(ph.run.items[0][1] > 0)
                        attention(pass_b[2 * r + y], ph.run)
                        if y:
                            ps = pass_b[2 * r + 1]
                            dve.wait_ge(st_done, ps.u0 + ps.units)
                            dve.wait_ge(oev_done, ps.u0 + ps.units + 2)
                            weights(1 + 2 * r)
                            weights(2 + 2 * r)
                            outputs_b(r)
                            if r:
                                decode(1)
                else:
                    if ph.kind != "up":
                        dve.wait_ge(ln_ax, KC * (n_norm + 1))
                    units_ahead(dve, ph, split, read)
                    if ph.kind != "up":
                        norm(n_norm, ph.next is None)
                        n_norm += 1
            for b in range(NBLK + 1):
                w = P if b < NBLK else SAMPLE
                dve.wait_ge(out_t, b + 1)
                dve.tensor_copy(yout[0:w, b, 512:1024], bank[2 * (b % 2) + 1][0:w, :]).then_inc(out_cv, 1)

        @block.gpsimd
        def _(pool):
            def scale_x(k):
                for c in range(KC):
                    pool.wait_ge(x_lo, KC * k + c + 1)
                    pool.tensor_scalar(z[:, c, :], z[:, c, :], ALPHA, None, ALU.mult).then_inc(ln_ax, 1)

            def hidden(ph):
                with pool.Fori(0, FC // 2) as it:
                    for b in range(2):
                        pool.wait_ge(acc_free[1], it * 2 + (ph.t0 // 2 + b + 3))
                        hi = hh[:, bass.ds(it * 2 + b, 1), :].rearrange("p o n -> p (o n)")
                        lo = hl[:, bass.ds(it * 2 + b, 1), :].rearrange("p o n -> p (o n)")
                        pool.tensor_copy(hi, h32[b][:]).then_inc(hh_rdy, 1)
                        pool.wait_ge(hh_rdy, it * 2 + (FC * ph.ffn + b + 1))
                        pool.tensor_tensor(lo, h32[b][:], hi.bitcast(F32), ALU.subtract).then_inc(hl_rdy, 1)

            def store_out(r, i):
                b, (gi, g, kind, p_) = i % 2, r.items[i]
                layer = r.layer
                pool.wait_ge(tr_free[b], (r.tr0 + i) // 2 + 3)
                col = (4 * r.rnd + p_) * P
                ss = r.R["ss"][b][:]
                if kind == "q" and layer == 0:
                    dst = q_d[0][:, 0, :].rearrange("s (g h r d) -> s g h r d", g=2, h=2, d=HD)[:, p_ // 4, :, p_ % 4, :]
                    pool.dma_start(dst, ss.rearrange("s (h d) -> s h d", h=2)).then_inc(ss_out[b], 16)
                elif kind == "q":
                    pool.dma_start(q_d[1][:, g, col:col + P], ss).then_inc(ss_out[b], 16)
                else:
                    pool.dma_start(kv_d[layer][:, g, int(kind == "v"), col:col + P], ss).then_inc(ss_out[b], 16)
                if kind == "q":
                    return
                w = int(kind == "v")
                dst = states_p[layer, g][0, 0].rearrange("r w h d -> r w (h d)")[:, w, col:col + P]
                if kind == "k":
                    src, s_ = r.R["kt"][b][:].rearrange("p (c n) -> p c n", c=NBLK), kt_out[b]
                else:
                    src, s_ = r.R["v"][gi][:, :, p_ * P:(p_ + 1) * P], v_out
                if g == 0:
                    pool.dma_start(dst, src[:, NBLK - 1, :]).then_inc(s_, 16)
                else:
                    pool.dma_start(dst.rearrange("(u c) n -> u c n", c=NBLK), src).then_inc(s_, 16)

            def run(ph):
                r = ph.run
                if ph is qkv[0] or ph is qkv[1, 0, 0]:
                    pool.wait_ge(ln_var, 2 * (norm_index(r.layer, 0) + 1))
                    for b in range(2):
                        pool.memset(r.R["qs"][b][:], 0.0)
                    pool.memset(r.R["st"][1][:], 0.0).then_inc(qs_zero, 1)
                    pool.wait_ge(qs_zero, r.layer + 1)
                else:
                    k = runs.index(r)
                    prev = PASS_OF[k - 1]
                    pool.wait_ge(sc_done, prev.u0 + prev.units + 2)
                for i, (gi, g, kind, p_) in enumerate(r.items):
                    if kind != "v":
                        pool.wait_ge(acc_free[i % 2], (ph.t0 + i) // 2 + 3)
                        pool.tensor_copy(r.R[kind][gi][:, p_, :], r.R["st"][i % 2][:, 0:SEQ]).then_inc(qk_cp, 1)
                    if i:
                        store_out(r, i - 1)
                store_out(r, r.n - 1)

            def attention(ps, rn):
                R = ps.R
                pool.wait_ge(qk_cp, rn.cp_total)

                def stage(i, blk):
                    b = blk % 2
                    pool.wait_ge(sc_done, i * 4 + (ps.u0 + blk + 1))
                    for g in range(2 if ps.dilated else 1):
                        for hd in range(2):
                            rows = slice(hd * HD, (hd + 1) * HD)
                            src = R["q"][g][rows, bass.ds(i, 1), blk * P:(blk + 1) * P].rearrange("p o n -> p (o n)")
                            last = pool.tensor_copy(R["qs"][b][rows, 2 * g + hd, :], src)
                    last.then_inc(qs_rdy, 1)
                skewed(pool, ps.pairs, [(stage, 0)])

            def exchange(ps):
                r = (ps.n - 1) // 2
                pool.wait_ge(st_done, ps.u0 + ps.units)
                pat = "(u c) e -> u c e" if ps.dilated else "(c u) e -> u c e"
                pool.dma_start(md_d[r, ps.slot].rearrange(pat, c=NBLK), RB["md"][ps.slot][:].rearrange("p b k h -> p b (k h)")).then_inc(md_out, 16)

            def fetch(r):
                pool.wait_ge(md_out, 32 * (r + 1))
                for y in range(2):
                    pat = "(u c) e -> u c e" if y else "(c u) e -> u c e"
                    pool.dma_start(RB["mo"][y][:].rearrange("p b k h -> p b (k h)"), md_d[r, 1 - y].rearrange(pat, c=NBLK)).then_inc(md_in, 16)

            def decode(layer):
                L = LAYER[layer]
                D, kv = L["D"], L["kv"]
                rep = HEADS // kv
                r = L["runs"][-1]
                if layer == 0:
                    pool.wait_ge(ot_v, PAIRS)
                else:
                    pool.wait_ge(sp_l, 2)
                pool.wait_ge(v_out, r.v_total)
                for b in range(2):
                    pool.wait_ge(kt_out[b], r.kt_total[b])
                    pool.wait_ge(ss_out[b], r.ss_total[b])
                pool.memset(D["q2"][:].bitcast(F32), 0.0).then_inc(d_zero, 1)
                pool.memset(D["p"][:], 0.0).then_inc(d_zero, 1)
                for g in range(L["G"]):
                    c = states_s[layer, g]
                    R_ = c.shape[2]
                    dst = c[0][:, R_ - DEC:R_].rearrange("n t w h d -> n t (w h d)")
                    src = kv_d[layer][:, g].rearrange("(n t) w f -> n t (w f)", t=DEC)
                    pool.dma_start(dst, src).then_inc(new_done, 16)
                for y in L["prod"]:
                    if y.by:
                        continue
                    pool.wait_ge(d_kv[y.tile.slot], y.tile.val)
                    pool.wait_ge(d_qb, y.k + 1)
                    if y.k >= 3:
                        pool.wait_ge(d_red, y.k - 2)
                    kk = D["kv"][y.tile.slot][:].rearrange("p (k d) -> p k d", d=HD)[:, :, None, :].to_broadcast([P, kv, rep, HD])
                    pool.tensor_tensor(D["pr"][y.slot][:].rearrange("p (k r d) -> p k r d", r=rep, d=HD), kk,
                                       D["qb"][y.slot][:].rearrange("p (k r d) -> p k r d", r=rep, d=HD), ALU.mult).then_inc(d_mult[0], 1)

            for s_, n_ in ((mm_done, 2), (acc_free[0], 2), (acc_free[1], 2), (wl_rdy, 4), (hl_rdy, 2), (tr_free[0], 2),
                           (tr_free[1], 2), (sc_done, 2), (sm_done, 2), (pt_done, 2), (ptc_done, 2), (pv_done, 2), (oev_done, 2)):
                pool.sem_inc(s_, n_)
            pool.memset(ones[:], 1.0 / D_MODEL).then_inc(setup, 1)
            scale_x(0)
            pool.wait_ge(line_o, 64)
            n_norm = 0
            for ph in phases:
                if ph.kind == "up":
                    hidden(ph)
                elif ph.kind in ("down", "wo"):
                    n_norm += 1
                    if ph.next:
                        scale_x(n_norm)
                else:
                    run(ph)
                    if ph is qkv[0]:
                        attention(pass_a, ph.run)
                        decode(0)
                    else:
                        r, y = ph.run.rnd, int(ph.run.items[0][1] > 0)
                        attention(pass_b[2 * r + y], ph.run)
                        exchange(pass_b[2 * r + y])
                        if y:
                            fetch(r)
                            if r:
                                decode(1)


_INS = ["x_prompt", "x_sample", "cache_a_kv", "cache_b1_kv", "cache_b2_kv", "cache_b3_kv", "rel_bias_table", "ln_gain",
        "ln_bias", "ffn_w_gate", "ffn_w_up", "ffn_w_down", "attn_a_w_qkv", "attn_a_w_o", "attn_a_sinks", "attn_b_w_qkv",
        "attn_b_w_o"]
_OUTS = [("y_prompt", (1, 512, 1024)), ("y_sample", (8, 4, 1024)), ("state_a_p", (1, 1, 128, 2, 4, 64)),
         ("state_b1_p", (1, 1, 128, 2, 16, 64)), ("state_b2_p", (1, 1, 512, 2, 16, 64)), ("state_b3_p", (1, 1, 512, 2, 16, 64)),
         ("state_a_s", (1, 8, 128, 2, 4, 64)), ("state_b1_s", (1, 8, 128, 2, 16, 64)), ("state_b2_s", (1, 8, 512, 2, 16, 64)),
         ("state_b3_s", (1, 8, 2048, 2, 16, 64))]


def constants():
    p = np.arange(P)[:, None] % 32
    return {"c_ident": np.eye(P, dtype=np.float32), "c_lines": one_hot_lines(), "c_dec": one_hot_decode(),
            "c_pick": ((np.arange(P)[:, None] % SAMPLE == np.arange(SAMPLE)[None]) & (np.arange(P)[:, None] < 2 * SAMPLE)).astype(np.float32),
            "c_mask_a": (p // 4 == np.arange(KV_A)[None]).astype(np.float32) * (p < HEADS),
            "c_mask_b": (p == np.arange(HEADS)[None]).astype(np.float32)}


def kernel(**inputs):
    import concourse.bacc as bacc
    from concourse.bass_utils import run_bass_kernel_spmd

    nc = bacc.Bacc("TRN2", target_bir_lowering=False, num_devices=1)
    arrays, t, o = {}, {}, {}
    for name, a in {**{n: inputs[n] for n in _INS}, **constants()}.items():
        a = np.ascontiguousarray(a)
        if name.startswith("c_"):
            a = a.astype(np.float32)
        arrays[f"in_{name}"] = a
        t[name] = nc.dram_tensor(f"in_{name}", a.shape, mybir.dt.from_np(a.dtype), kind="ExternalInput").ap()
    for name, shape in _OUTS:
        o[name] = nc.dram_tensor(f"out_{name}", shape, F32, kind="ExternalOutput").ap()
    build(nc, t, o)
    r = run_bass_kernel_spmd(nc, [arrays], core_ids=[0])
    return tuple(r.results[0][f"out_{name}"] for name, _ in _OUTS)
```

```python
from contextlib import ExitStack

import numpy as np

import concourse.bass as bass
from concourse import mybir

F32 = mybir.dt.float32
F32R = mybir.dt.float32r
ALU = mybir.AluOpType
ACT = mybir.ActivationFunctionType
AX_X = mybir.AxisListType.X

P = 128
D_MODEL = 1024
KC = D_MODEL // P
SEQ = 512
NS = 8
DEC = 4
SAMPLE = NS * DEC
TOK = SEQ + SAMPLE
HALF = TOK // 2
D_FF = ((8 * D_MODEL // 3 + 127) // 128) * 128
FC = D_FF // P
FU = FC // 2
DEPTH = 2
HEADS = 16
HD = 64
PAIRS = HEADS // 2
KV_A = 4
ALPHA = (2 * DEPTH) ** 0.25
LN_EPS = 1e-5
SCALE = HD ** -0.5
NEG = -1e30
BLK = 128
NBLK = SEQ // BLK
DILATION = (1, 4, 16)
NUM_BUCKETS = 32
MAX_DISTANCE = 2048
QKV_A = (HEADS + 2 * KV_A) * HD
RAW = 4
KV_SLOTS = 7
LINE_X, LINE_Y = 384, 256
LINES = LINE_X + 2 * LINE_Y


def bucket(dist):
    exact = NUM_BUCKETS // 2
    d = np.maximum(dist.astype(np.float32), np.float32(1.0))
    large = exact + (np.log(d / np.float32(exact)) / np.float32(np.log(MAX_DISTANCE / exact))
                     * np.float32(NUM_BUCKETS - exact)).astype(np.int32)
    return np.where(dist < exact, dist, np.minimum(large, NUM_BUCKETS - 1))


def one_hot_lines():
    out = np.zeros((NUM_BUCKETS + 1, LINES), np.float32)

    def put(col, dist, valid):
        b = bucket(np.maximum(dist, 0))
        for c, bb, ok in zip(col, b, valid):
            if ok:
                out[bb, c] = 1.0
            else:
                out[NUM_BUCKETS, c] = NEG
    j = np.arange(LINE_X)
    rel = 2 * BLK - 1 - j
    put(j, rel, (rel >= 0) & (rel <= BLK))
    j = np.arange(LINE_Y)
    rel = BLK - 1 - j
    put(LINE_X + j, rel * 4, rel >= 0)
    put(LINE_X + LINE_Y + j, rel * 4, (rel >= 0) & (rel % 4 == 0))
    return out


def one_hot_decode():
    n0 = BLK + DEC - 1
    out = np.zeros((NUM_BUCKETS + 1, n0 + 2 * BLK + 2 * DEC), np.float32)

    def put(c, dist, ok):
        if ok:
            out[int(bucket(np.array([dist]))[0]), c] = 1.0
        else:
            out[NUM_BUCKETS, c] = NEG
    for j in range(n0):
        dist = BLK - (j - (DEC - 1))
        put(j, dist, 0 <= dist <= BLK)
    for g in (1, 2):
        for i in range(BLK):
            put(n0 + (g - 1) * BLK + i, (BLK - i) * DILATION[g], True)
    for j in range(2 * DEC - 1):
        dist = DEC - 1 - j
        put(n0 + 2 * BLK + j, dist, dist >= 0)
    put(n0 + 2 * BLK + 2 * DEC - 1, 0, True)
    return out


def build(nc, t, o):
    oh_lines, oh_dec = t["c_lines"], t["c_dec"]
    ND = oh_dec.shape[1]
    N0 = BLK + DEC - 1
    with ExitStack() as ctx:
        def sem(name):
            return ctx.enter_context(nc.semaphore(name))

        def sb(name, shape, dt=F32, scope=None):
            return (scope or ctx).enter_context(nc.sbuf_tensor("sb_" + name, shape, dt))

        def dram(name, shape):
            return nc.dram_tensor("scr_" + name, shape, F32, kind="Internal").ap()

        lines_d = [dram("lines_x", [HEADS, P, LINE_X]), dram("lines_y0", [HEADS, P, LINE_Y]), dram("lines_y1", [HEADS, P, LINE_Y])]
        once_d = dram("lines", [HEADS, LINES])
        dec_lines_d = dram("dec_lines", [HEADS, ND])
        q_d = {0: dram("qa", [SAMPLE, 1, D_MODEL]), 1: dram("qb", [SAMPLE, 3, D_MODEL])}
        kv_d = {0: dram("kva", [SAMPLE, 1, 2, KV_A * HD]), 1: dram("kvb", [SAMPLE, 3, 2, D_MODEL])}
        md_d = dram("md", [2, 2, SEQ, 2 * PAIRS])
        snew_d = {0: dram("snew_a", [SAMPLE * HEADS, DEC]), 1: dram("snew_b", [SAMPLE * HEADS, DEC + 2])}
        pnew_d = {0: dram("pnew_a", [SAMPLE * HEADS, DEC]), 1: dram("pnew_b", [SAMPLE * HEADS, DEC + 2])}
        odec_d = {0: dram("odec_a", [SAMPLE, D_MODEL]), 1: dram("odec_b", [SAMPLE, D_MODEL])}

        z = sb("z", [P, KC, TOK])
        xh = sb("xh", [P, KC, TOK], F32R)
        xl = sb("xl", [P, KC, TOK], F32R)
        raw = [sb(f"raw{i}", [P, FU, P]) for i in range(RAW)]
        wh = [sb(f"wh{i}", [P, FU, P], F32R) for i in range(2)]
        wl = [sb(f"wl{i}", [P, FU, P], F32R) for i in range(2)]
        ident = sb("ident", [P, P])
        ones = sb("ones", [P, P])
        zeros = sb("zeros", [P, P])
        pick32 = sb("pick32", [P, SAMPLE])
        pick = sb("pick", [P, SAMPLE], F32R)
        gain = sb("gain", [P, 3 * DEPTH, KC])
        shift = sb("shift", [P, 3 * DEPTH, KC])
        rstd = sb("rstd", [P, TOK])

        dec_const = []
        for n, G, kv, new in (("a", 1, KV_A, DEC), ("b", 3, HEADS, DEC + 2)):
            dec_const.append({"bc": sb(f"dbc{n}", [P, G, P]), "bn": sb(f"dbn{n}", [P, new]), "snk": sb(f"dsnk{n}", [P, 1]),
                              "mask": sb(f"dmask{n}", [P, kv])})

        with ExitStack() as s:
            hh = sb("hh", [P, FC, TOK], F32R, s)
            hl = sb("hl", [P, FC, TOK], F32R, s)
            sil = [sb(f"sil{i}", [P, TOK], F32, s) for i in range(2)]
            h32 = [sb(f"h32{i}", [P, TOK], F32, s) for i in range(2)]
        with ExitStack() as s:
            sq = sb("sq", [P, KC, TOK], F32, s)
        with ExitStack() as s:
            xin = sb("xin", [P, NBLK, D_MODEL], F32, s)
            xsin = sb("xsin", [SAMPLE, D_MODEL], F32, s)
            tab = sb("tab", [NUM_BUCKETS + 1, HEADS], F32, s)
            oh1 = sb("oh1", [NUM_BUCKETS + 1, LINES], F32, s)
            oh2 = sb("oh2", [NUM_BUCKETS + 1, ND], F32, s)
            lin1 = sb("lin1", [HEADS, LINES], F32, s)
            lin2 = sb("lin2", [HEADS, ND], F32, s)
        with ExitStack() as s:
            yout = sb("yout", [P, NBLK + 1, D_MODEL], F32, s)

        def attn_common(s, n, heads):
            r = {}
            r["st"] = [sb(f"st{n}{i}", [P, TOK], F32, s) for i in range(2)]
            r["kt"] = [sb(f"kt{n}{i}", [P, NBLK * P], F32, s) for i in range(2)]
            r["ss"] = [sb(f"ss{n}{i}", [SAMPLE, P], F32, s) for i in range(2)]
            r["qs"] = [sb(f"qs{n}{i}", [P, 4, P], F32, s) for i in range(2)]
            r["bias"] = sb(f"bias{n}", [P, heads, 2 * BLK], F32, s)
            for m in ("nm", "dn"):
                r[m] = [sb(f"{m}{n}{i}", [P, 2], F32, s) for i in range(2)]
            return r

        with ExitStack() as s:
            RA = attn_common(s, "a", HEADS)
            RA["q"] = [sb("qa", [P, PAIRS, SEQ], F32, s)]
            RA["k"] = [sb("ka", [P, 2, SEQ], F32, s)]
            RA["v"] = [sb("va", [P, NBLK, KV_A * HD], F32, s)]
            RA["o"] = [sb("oa", [P, NBLK, HEADS * HD], F32, s)]
            RA["md"] = [sb("mda", [P, NBLK, 2, HEADS], F32, s)]
            RA["mo"] = [sb("moa", [P, NBLK, 2, HEADS], F32, s)]
            RA["sink"] = sb("sinka", [P, HEADS], F32, s)
            RA["t"] = [sb(f"ta{i}", [P, NBLK, HEADS], F32, s) for i in range(5)]
        with ExitStack() as s:
            RB = attn_common(s, "b", PAIRS)
            for m in ("q", "k"):
                RB[m] = [sb(f"{m}b{i}", [P, 4, SEQ], F32, s) for i in range(2)]
            RB["v"] = [sb(f"vb{i}", [P, NBLK, SEQ], F32, s) for i in range(2)]
            RB["o"] = [sb(f"ob{i}", [P, NBLK, SEQ], F32, s) for i in range(2)]
            RB["md"] = [sb(f"mdb{i}", [P, NBLK, 2, PAIRS], F32, s) for i in range(2)]
            RB["mo"] = [sb(f"mob{i}", [P, NBLK, 2, PAIRS], F32, s) for i in range(2)]
            RB["t"] = [sb(f"tb{i}", [P, NBLK, PAIRS], F32, s) for i in range(5)]
            RB["at"] = sb("at", [P, 4, SEQ], F32, s)

        def decode_regime(s, n, G, kv, new):
            r = dict(dec_const["ab".index(n)])
            r["kv"] = [sb(f"dkv{n}{i}", [P, kv * HD], F32, s) for i in range(KV_SLOTS)]
            r["qb"] = [sb(f"dqb{n}{i}", [P, D_MODEL], F32, s) for i in range(3)]
            r["pr"] = [sb(f"dpr{n}{i}", [P, D_MODEL], F32, s) for i in range(3)]
            r["s"] = sb(f"ds{n}", [P, G, SAMPLE * HEADS], F32, s)
            r["p"] = sb(f"dp{n}", [P, G, SAMPLE, HEADS], F32, s)
            r["sm"] = [sb(f"dsm{n}{i}", [P, G * P + new + 1], F32, s) for i in range(2)]
            r["snew"] = sb(f"dsn{n}", [SAMPLE, HEADS, new], F32, s)
            r["snb"] = sb(f"dsnb{n}", [P, 4, new], F32, s)
            r["pnb"] = sb(f"dpnb{n}", [P, 4, new], F32, s)
            r["pn"] = sb(f"dpn{n}", [SAMPLE, HEADS, new], F32, s)
            r["st"] = sb(f"dst{n}", [P, 4, 4], F32, s)
            r["qn"] = sb(f"dqn{n}", [2 * SAMPLE, G, D_MODEL], F32, s)
            r["q2"] = sb(f"dq2{n}", [P, G, D_MODEL], F32R, s)
            r["kn"] = [sb(f"dkn{n}{i}", [SAMPLE, kv * HD], F32, s) for i in range(2)]
            r["oc"] = sb(f"doc{n}", [P, NS, HD], F32, s)
            r["ot"] = sb(f"dot{n}", [P, D_MODEL], F32, s)
            return r
        with ExitStack() as s:
            DA = decode_regime(s, "a", 1, KV_A, DEC)
        with ExitStack() as s:
            DB = decode_regime(s, "b", 3, HEADS, DEC + 2)

        bank = [ctx.enter_context(nc.psum_tensor(f"bank{i}", [P, 512], F32)) for i in range(8)]

        raw_in = [sem(f"raw_in{i}") for i in range(RAW)]
        wh_rdy, wl_rdy = sem("wh_rdy"), sem("wl_rdy")
        mm_done = sem("mm_done")
        acc_free = [sem(f"acc_free{i}") for i in range(2)]
        hh_rdy, hl_rdy = sem("hh_rdy"), sem("hl_rdy")
        ln_mean, ln_dev, ln_sq, ln_var, ln_rs, ln_nrm = (sem("ln_" + n) for n in ("mean", "dev", "sq", "var", "rs", "nrm"))
        ln_aff, x_hi, x_lo, ln_ax = (sem(n) for n in ("ln_aff", "x_hi", "x_lo", "ln_ax"))
        in_ld, cst_ld, norm_ld, setup, init_t, line_t, line_c, line_o, line_x = (
            sem(n) for n in ("in_ld", "cst_ld", "norm_ld", "setup", "init_t", "line_t", "line_c", "line_o", "line_x"))
        tr_done = sem("tr_done")
        tr_free = [sem(f"tr_free{i}") for i in range(2)]
        qk_cp = sem("qk_cp")
        kt_out = [sem(f"kt_out{i}") for i in range(2)]
        ss_out = [sem(f"ss_out{i}") for i in range(2)]
        v_out = sem("v_out")
        qs_zero, qs_rdy = sem("qs_zero"), sem("qs_rdy")
        sc_done, sm_done, nm_done, ex_done, pt_done, ptc_done, pv_done, oev_done = (
            sem(n) for n in ("sc_done", "sm_done", "nm_done", "ex_done", "pt_done", "ptc_done", "pv_done", "oev_done"))
        bias_ld, md_out, md_in, cmb_v, cmb_a, cmb_r, ow_rdy, st_done, sink_rdy, d_sx, d_sum, ln_root = (
            sem(n) for n in ("bias_ld", "md_out", "md_in", "cmb_v", "cmb_a", "cmb_r", "ow_rdy", "st_done", "sink_rdy", "d_sx", "d_sum", "ln_root"))
        ot_done, ot_a, ot_v, sp_h, sp_l = (sem(n) for n in ("ot_done", "ot_a", "ot_v", "sp_h", "sp_l"))
        d_kv = [sem(f"d_kv{i}") for i in range(KV_SLOTS)]
        d_qp, d_qb = sem("d_qp"), sem("d_qb")
        d_mult = [sem("d_mult_pool"), sem("d_mult_dve")]
        d_kn = [sem(f"d_kn{i}") for i in range(2)]
        (d_cst, d_qn, d_q2, d_q2l, d_add, d_red, d_nv, d_sn_out, d_sn_in, d_st, d_sv, d_nm, d_ex, d_pt, d_ptc, d_pn_out, d_pn_in,
         d_pv, d_msk, d_oc, d_oc_out, d_ot_in, d_tt, d_ta, d_tv, d_zero) = (
            sem("d_" + n) for n in ("cst", "qn", "q2", "q2l", "add", "red", "nv", "sn_out", "sn_in", "st", "sv", "nm", "ex", "pt",
                                    "ptc", "pn_out", "pn_in", "pv", "msk", "oc", "oc_out", "ot_in", "tt", "ta",
                                    "tv", "zero"))
        out_t, out_ca, out_cv, out_done, new_done = (sem(n) for n in ("out_t", "out_ca", "out_cv", "out_done", "new_done"))
        copy_done = [sem(f"copy_done{i}") for i in range(5)]

        class Phase:
            def __init__(self, kind, units, chunks, dmas=1, l=None, f=None, ffn=None):
                self.kind, self.units, self.chunks, self.dmas = kind, units, chunks, dmas
                self.l, self.f, self.ffn = l, f, ffn

        phases = []

        def add(*a, **kw):
            ph = Phase(*a, **kw)
            if phases:
                q = phases[-1]
                q.next = ph
                ph.u0, ph.t0 = q.u0 + q.units, q.t0 + q.tiles
                ph.land0 = [x + 16 * q.dmas * (q.units // RAW) for x in q.land0]
            else:
                ph.u0, ph.t0, ph.land0 = 0, 0, [0] * RAW
            ph.tiles = ph.units // 2 if ph.kind == "down" else ph.units
            ph.next = None
            phases.append(ph)
            return ph

        up, down, qkv, wo = {}, {}, {}, {}
        for l in range(DEPTH):
            for f in range(2):
                up[l, f] = add("up", 2 * FC, KC, l=l, f=f, ffn=2 * l + f)
                down[l, f] = add("down", 2 * KC, FU, l=l, f=f, ffn=2 * l + f)
                if f == 0 and l == 0:
                    qkv[0] = add("qkv", 12, KC, dmas=2)
                    wo[0] = add("wo", KC, KC, dmas=4)
                elif f == 0:
                    for r in range(2):
                        qkv[1, r, 0] = add("qkv", 12, KC)
                        qkv[1, r, 1] = add("qkv", 24, KC)
                    wo[1] = add("wo", KC, KC)

        def acc(s, h):
            return bank[2 * s + h][:, 0:HALF]

        halves = [slice(0, HALF), slice(HALF, TOK)]

        class Run:
            pass
        runs = []

        def add_run(ph, layer, rnd, groups):
            r = Run()
            r.ph, r.layer, r.rnd, r.n = ph, layer, rnd, ph.units
            r.tr0 = sum(x.n for x in runs)
            r.items = []
            for gi, g in enumerate(groups):
                for kind, cnt in (("q", PAIRS if layer == 0 else 4), ("k", 2 if layer == 0 else 4),
                                  ("v", 2 if layer == 0 else 4)):
                    r.items += [(gi, g, kind, p) for p in range(cnt)]
            r.R = RA if layer == 0 else RB
            runs.append(r)
            ph.run = r
            return r
        run_a = add_run(qkv[0], 0, 0, [0])
        run_b = [[add_run(qkv[1, r, 0], 1, r, [0]), add_run(qkv[1, r, 1], 1, r, [1, 2])] for r in range(2)]

        class Pass:
            def __init__(self, n, R, pairs, first, dilated, slot):
                self.n, self.R, self.pairs, self.u0, self.dilated, self.slot = n, R, pairs, first, dilated, slot
                self.units = 4 * pairs
        pass_a = Pass(0, RA, PAIRS, 0, False, 0)
        pass_b = []
        nu = pass_a.units
        for r in range(2):
            for y in range(2):
                pass_b.append(Pass(1 + 2 * r + y, RB, 4, nu, bool(y), y))
                nu += 16

        def skewed(eng, n_pairs, stages):
            last = max(lag for _, lag in stages)
            for s_ in range(4):
                for fn, lag in stages:
                    if s_ >= lag:
                        fn(0, s_ - lag)
            with eng.Fori(1, n_pairs) as i:
                for s_ in range(4):
                    for fn, lag in stages:
                        fn(i + (s_ - lag) // 4, (s_ - lag) % 4)
            for s_ in range(last):
                for fn, lag in stages:
                    if s_ < lag:
                        fn(n_pairs - 1, 4 + s_ - lag)

        def first_col(ps, blk):
            return BLK if (not ps.dilated and blk == 0) else 0

        LAYER = {0: dict(G=1, kv=KV_A, new=DEC, D=DA, ps=pass_a, runs=[run_a]),
                 1: dict(G=3, kv=HEADS, new=DEC + 2, D=DB, ps=pass_b[-1], runs=run_b[0] + run_b[1])}
        caches = {(0, 0): t["cache_a_kv"], (1, 0): t["cache_b1_kv"], (1, 1): t["cache_b2_kv"], (1, 2): t["cache_b3_kv"]}
        states_p = {(0, 0): o["state_a_p"], (1, 0): o["state_b1_p"], (1, 1): o["state_b2_p"], (1, 2): o["state_b3_p"]}
        states_s = {(0, 0): o["state_a_s"], (1, 0): o["state_b1_s"], (1, 1): o["state_b2_s"], (1, 2): o["state_b3_s"]}

        count = {"kt": [0, 0], "ss": [0, 0], "cp": 0, "v": 0}
        for r in runs:
            r.kt_before, r.ss_before, r.cp_after, r.cp0 = [], [], [], count["cp"]
            for i, (gi, g, kind, p_) in enumerate(r.items):
                b = i % 2
                r.kt_before.append(count["kt"][b])
                r.ss_before.append(count["ss"][b])
                count["ss"][b] += 16
                if kind == "k":
                    count["kt"][b] += 16
                if kind == "v":
                    count["v"] += 16
                else:
                    count["cp"] += 1
                r.cp_after.append(count["cp"])
            r.kt_total, r.ss_total, r.v_total, r.cp_total = list(count["kt"]), list(count["ss"]), count["v"], count["cp"]

        def new_cols(layer):
            c = [(0, t_) for t_ in range(DEC)]
            return c if layer == 0 else c + [(1, None), (2, None)]

        def dec_tiles(layer):
            out = []
            for n in range(NS):
                out.append((n, 0, tuple(range(DEC))))
                for g in range(1, LAYER[layer]["G"]):
                    out += [(n, g, (tau,)) for tau in range(DEC)]
            return out

        class Load:
            def __init__(self, ring, slots, what):
                self.i = len(ring)
                self.slot = self.i % slots
                self.val = 16 * (self.i // slots + 1)
                self.landed = None
                self.what = what
                self.done = None
                self.prev = ring[self.i - slots] if self.i >= slots else None
                ring.append(self)

        class Product:
            def __init__(self, k, n, g, tau, tile, mult):
                self.k, self.slot, self.n, self.g, self.tau, self.tile = k, k % 3, n, g, tau, tile
                self.by = int(self.slot == 2)
                mult[self.by] += 1
                self.mult = (d_mult[self.by], mult[self.by])

        LAG = 2

        def keys_at(L, p_):
            return L["k"][p_] if p_ < len(L["k"]) else None

        def values_at(L, p_):
            return L["v"][p_ - L["per"] - LAG] if p_ >= L["per"] + LAG else None

        def new_value_at(L, i):
            return min(L["end"] - 1, 4 * L["per"] + 6 + 2 * i)

        def part_at(L, p_, after):
            q = p_ - after
            return q // L["per"] - 1 if q >= L["per"] and q % L["per"] == 0 and q // L["per"] <= 4 else None
        kv_ring, kn_ring = [], []
        mult = [0, 0]
        n_prod = n_pv = n_nv = 0
        for layer in range(2):
            L = LAYER[layer]
            L["kn"], L["k"], L["prod"], L["v"], L["vn"] = [], [], [], [], []
            L["nv0"] = n_nv
            for c_, (g, tp) in enumerate(new_cols(layer)):
                x = Load(kn_ring, 2, (c_, g, tp))
                n_nv += 2
                x.done = [(d_nv, n_nv)]
                L["kn"].append(x)
            tiles = dec_tiles(layer)
            L["per"] = len(tiles) // 4
            L["end"] = len(tiles) + L["per"] + LAG
            for p_ in range(L["end"]):
                if p_ < len(tiles):
                    x = Load(kv_ring, KV_SLOTS, tiles[p_])
                    L["k"].append(x)
                    n, g, taus = x.what
                    x.prods = []
                    for tau in taus:
                        x.prods.append(Product(n_prod, n, g, tau, x, mult))
                        n_prod += 1
                    L["prod"] += x.prods
                    x.done = [(d_mult[e], mult[e]) for e in range(2) if mult[e]]
                if p_ >= L["per"] + LAG:
                    x = Load(kv_ring, KV_SLOTS, tiles[p_ - L["per"] - LAG])
                    L["v"].append(x)
                    n_pv += 1
                    x.done = [(d_pv, n_pv)]
            for c_, (g, tp) in enumerate(new_cols(layer)):
                x = Load(kn_ring, 2, (c_, g, tp))
                n_nv += 2
                x.done = [(d_nv, n_nv)]
                L["vn"].append(x)
        landed_ = [0, 0]
        for x in kn_ring:
            landed_[x.slot] += 16
            x.landed = landed_[x.slot]
        BIAS_LD = {0: 16 * 8}
        for ps in pass_b:
            BIAS_LD[ps.n] = BIAS_LD[ps.n - 1] + (32 if ps.dilated else 16)
        PASS_OF = [pass_a] + pass_b
        cst_dmas = {0: 3 * 2 * DEC + 1, 1: 5 * 2 * DEC + 1}

        UP_ITS, DOWN_ITS = 2 * FC // RAW, 2 * KC // RAW
        B3_KEEP, B2_KEEP = DILATION[2] * BLK - DEC, DILATION[1] * BLK - DEC
        UP_ROWS = 88
        DOWN_ROWS = (B3_KEEP - UP_ITS * 2 * UP_ROWS) // DOWN_ITS
        B2_ROWS = B2_KEEP // DOWN_ITS
        assert UP_ITS * 2 * UP_ROWS + DOWN_ITS * DOWN_ROWS == B3_KEEP and DOWN_ITS * B2_ROWS == B2_KEEP

        def norm_index(layer, j):
            return 3 * layer + j

        block = ctx.enter_context(nc.Block())

        @block.sync
        def _(sp):
            sp.dma_start(ident[:], t["c_ident"]).then_inc(cst_ld, 16)
            sp.dma_start(pick32[:], t["c_pick"]).then_inc(cst_ld, 16)
            sp.dma_start(tab[0:NUM_BUCKETS, :], t["rel_bias_table"]).then_inc(cst_ld, 16)
            sp.dma_start(oh1[:], oh_lines).then_inc(cst_ld, 16)
            sp.dma_start(oh2[:], oh_dec).then_inc(cst_ld, 16)
            sp.dma_start(xin[:], t["x_prompt"][0].rearrange("(b p) d -> p b d", p=P)).then_inc(in_ld, 16)
            sp.dma_start(xsin[:], t["x_sample"].rearrange("n t d -> (n t) d")).then_inc(in_ld, 16)

            def keep_rows(g, n, r0, rows, f):
                src = caches[1, g][0, n].rearrange("r w h d -> r (w h d)")[bass.ds(r0 + DEC, rows), :]
                dst = states_s[1, g][0, n].rearrange("r w h d -> r (w h d)")[bass.ds(r0, rows), :]
                sp.dma_start(dst, src).then_inc(copy_done[f], 16)

            def keep_small(layer, n0, n1):
                src = caches[layer, 0][0, n0:n1].rearrange("n r w h d -> n (r w h d)")
                dst = states_s[layer, 0][0, n0:n1].rearrange("n r w h d -> n (r w h d)")
                row = 2 * LAYER[layer]["kv"] * HD
                total = src.shape[1]
                sp.dma_start(dst[:, 0:total - DEC * row], src[:, DEC * row:total]).then_inc(copy_done[2 * DEPTH], 16)

            def load_unit(ph, it, j):
                sp.wait_ge(wl_rdy, it * RAW + (ph.u0 + j + 1))
                if ph.kind == "up":
                    w = t["ffn_w_gate" if j % 2 == 0 else "ffn_w_up"][ph.l, ph.f]
                    src = w.rearrange("(c p) (f n) -> p c f n", p=P, n=P)[:, :, bass.ds(it * 2 + j // 2, 1), :]
                    sp.dma_start(raw[j][:, 0:KC, :], src.rearrange("p c f n -> p c (f n)")).then_inc(raw_in[j], 16)
                elif ph.kind == "down":
                    w = t["ffn_w_down"][ph.l, ph.f].rearrange("(u c p) (m n) -> p u c m n", p=P, n=P, u=2)
                    src = w[:, j % 2, :, bass.ds(it * 2 + j // 2, 1), :]
                    sp.dma_start(raw[j][:], src.rearrange("p c m n -> p c (m n)")).then_inc(raw_in[j], 16)
                elif ph.kind == "qkv":
                    r = ph.run
                    w = t["attn_b_w_qkv"][0].rearrange("(c p) (k r j n) -> p c k r j n", p=P, r=2, j=4, n=P)
                    src = w[:, :, bass.ds(it + 3 * r.items[0][1], 1), r.rnd, j, :]
                    sp.dma_start(raw[j][:, 0:KC, :], src.rearrange("p c k n -> p c (k n)")).then_inc(raw_in[j], 16)
                elif ph.dmas == 1:
                    w = t["attn_b_w_o"][0].rearrange("(c p) (m n) -> p c m n", p=P, n=P)
                    src = w[:, :, bass.ds(it * RAW + j, 1), :]
                    sp.dma_start(raw[j][:, 0:KC, :], src.rearrange("p c m n -> p c (m n)")).then_inc(raw_in[j], 16)
                else:
                    w = t["attn_a_w_o"][0].rearrange("(g h r d) (m n) -> g h d r m n", g=2, h=2, d=HD, n=P)
                    for g in range(2):
                        for h in range(2):
                            src = w[g, h][:, :, bass.ds(it * RAW + j, 1), :].rearrange("d r m n -> d r (m n)")
                            sp.dma_start(raw[j][h * HD:(h + 1) * HD, 4 * g:4 * g + 4, :], src).then_inc(raw_in[j], 16)

            def load_units(ph, first):
                with sp.Fori(first, ph.units // RAW) as it:
                    for j in range(RAW):
                        load_unit(ph, it, j)
                        if ph.kind == "up":
                            keep_rows(2, 2 * ph.ffn + j % 2, it * (2 * UP_ROWS) + (j // 2) * UP_ROWS, UP_ROWS, ph.ffn)
                        elif ph.kind == "down" and j < 2:
                            keep_rows(1, 2 * ph.ffn + j % 2, it * B2_ROWS, B2_ROWS, ph.ffn)
                        elif ph.kind == "down":
                            keep_rows(2, 2 * ph.ffn + j % 2, it * DOWN_ROWS + UP_ITS * 2 * UP_ROWS, DOWN_ROWS, ph.ffn)

            def load_first(ph):
                for j in range(RAW):
                    load_unit(ph, 0, j)

            def load_qkv_a(ph, units):
                w = t["attn_a_w_qkv"][0].rearrange("(c p) n -> p c n", p=P)
                for i in units:
                    gi, g, kind, p_ = ph.run.items[i]
                    sp.wait_ge(wl_rdy, ph.u0 + i + 1)
                    for h in range(2):
                        if kind == "q":
                            col = ((p_ // 4) * 8 + h * 4 + p_ % 4) * HD
                        else:
                            col = (HEADS + (KV_A if kind == "v" else 0) + 2 * p_ + h) * HD
                        sp.dma_start(raw[i % RAW][:, 0:KC, h * HD:(h + 1) * HD], w[:, :, col:col + HD]).then_inc(raw_in[i % RAW], 16)

            def load_bias(ps):
                R = ps.R

                def toeplitz(l, h0, n, width):
                    W = lines_d[l].shape[2]
                    return bass.AP(lines_d[l].tensor, h0 * P * W + BLK - 1, [[W - 1, P], [P * W, n], [1, width]])

                if ps is pass_a or ps is pass_b[0]:
                    sp.wait_ge(ln_var, 2 * (norm_index(0 if ps is pass_a else 1, 0) + 1))
                else:
                    sp.wait_ge(sm_done, ps.u0 + 2)
                if ps is pass_a:
                    sp.wait_ge(line_x, 48)
                    for g in range(2):
                        for h in range(2):
                            dst = R["bias"][:].rearrange("p (g r h) k -> p g h r k", g=2, h=2)[:, g, h]
                            sp.dma_start(dst, toeplitz(0, g * 8 + h * 4, 4, 2 * BLK)).then_inc(bias_ld, 16)
                            with nc.allow_non_contiguous_dma(reason="4 sinks"):
                                dst = R["sink"][:].rearrange("p (g r h) -> p g h r", g=2, h=2)[:, g, h]
                                src = t["attn_a_sinks"][0:1, g * 8 + h * 4:g * 8 + h * 4 + 4]
                                sp.dma_start(dst, src.to_broadcast([P, 4])).then_inc(bias_ld, 16)
                else:
                    h0 = (ps.n - 1) // 2 * 8
                    if not ps.dilated:
                        sp.dma_start(R["bias"][:], toeplitz(0, h0, 8, 2 * BLK)).then_inc(bias_ld, 16)
                    else:
                        for g in range(2):
                            sp.dma_start(R["bias"][:, :, g * BLK:(g + 1) * BLK], toeplitz(1 + g, h0, 8, BLK)).then_inc(bias_ld, 16)

            def cached(layer, n, g, tau, which):
                c = caches[layer, g][0, n]
                if g == 0:
                    return c[:, which].rearrange("r h d -> r (h d)")
                return c.rearrange("(i e) w h d -> e i w (h d)", e=DILATION[g])[tau, :, which]

            def slot_free(x):
                if x.prev:
                    for s_, val in x.prev.done:
                        sp.wait_ge(s_, val)

            def load_new(layer, x, which):
                D, (c_, g, tp) = LAYER[layer]["D"], x.what
                slot_free(x)
                dst = D["kn"][x.slot][:]
                if tp is None:
                    sp.dma_start(dst, kv_d[layer][:, g, which, :]).then_inc(d_kn[x.slot], 16)
                else:
                    rows = kv_d[layer].rearrange("(n t) g w f -> n t g w f", t=DEC)[:, tp, g, which, :]
                    src = rows[:, None, :].to_broadcast([NS, DEC, rows.shape[1]])
                    sp.dma_start(dst, src).then_inc(d_kn[x.slot], 16)

            def load_norms():
                with nc.allow_non_contiguous_dma(reason="feature on partition, a few values each"):
                    for n_ in range(3 * DEPTH):
                        sp.dma_start(gain[:, n_, :], t["ln_gain"][n_ // 3, n_ % 3].rearrange("(c p) -> p c", p=P)).then_inc(norm_ld, 16)
                        sp.dma_start(shift[:, n_, :], t["ln_bias"][n_ // 3, n_ % 3].rearrange("(c p) -> p c", p=P)).then_inc(norm_ld, 16)

            def repeat_lines():
                sp.wait_ge(line_o, 32)
                for l, c0 in enumerate((0, LINE_X, LINE_X + LINE_Y)):
                    W = lines_d[l].shape[2]
                    sp.dma_start(lines_d[l], once_d[:, None, c0:c0 + W].to_broadcast([HEADS, P, W])).then_inc(line_x, 16)

            def load_decode_constants(layer):
                D = LAYER[layer]["D"]
                sp.wait_ge(line_o, 32)
                with nc.allow_non_contiguous_dma(reason="one value per partition"):
                    for tau in range(DEC):
                        for n2 in range(2):
                            rows = slice((n2 * DEC + tau) * HEADS, (n2 * DEC + tau + 1) * HEADS)
                            c0 = DEC - 1 - tau
                            sp.dma_start(D["bc"][rows, 0, :], dec_lines_d[:, c0:c0 + BLK]).then_inc(d_cst, 16)
                            c0 += N0 + 2 * BLK
                            sp.dma_start(D["bn"][rows, 0:DEC], dec_lines_d[:, c0:c0 + DEC]).then_inc(d_cst, 16)
                            if layer:
                                src = dec_lines_d[:, N0:N0 + 2 * BLK].rearrange("h (g r) -> h g r", g=2)
                                sp.dma_start(D["bc"][rows, 1:3, :], src).then_inc(d_cst, 16)
                                for c_ in range(2):
                                    sp.dma_start(D["bn"][rows, DEC + c_:DEC + c_ + 1], dec_lines_d[:, ND - 1:ND]).then_inc(d_cst, 16)
                            else:
                                sp.dma_start(D["snk"][rows, :], t["attn_a_sinks"].rearrange("o h -> h o")).then_inc(d_cst, 16)
                sp.dma_start(D["mask"][:], t["c_mask_b" if layer else "c_mask_a"]).then_inc(d_cst, 16)

            def load_decode(layer):
                L = LAYER[layer]
                D = L["D"]
                sp.wait_ge(d_zero, 2 * layer + 1)
                for k in range(2):
                    sp.dma_start(D["qn"][k * SAMPLE:(k + 1) * SAMPLE], q_d[layer]).then_inc(d_qn, 16)
                def load_cached(x, which):
                    n, g, taus = x.what
                    slot_free(x)
                    sp.dma_start(D["kv"][x.slot][:], cached(layer, n, g, taus[0], which)).then_inc(d_kv[x.slot], 16)
                for p_ in range(L["end"]):
                    if keys_at(L, p_):
                        load_cached(keys_at(L, p_), 0)
                    for x in L["kn"][2 * p_:2 * p_ + 2]:
                        load_new(layer, x, 0)
                    if values_at(L, p_):
                        load_cached(values_at(L, p_), 1)
                    for i, x in enumerate(L["vn"]):
                        if p_ == new_value_at(L, i):
                            load_new(layer, x, 1)

            peeled = 0
            for ph in phases:
                if ph is qkv[0]:
                    load_qkv_a(ph, range(RAW))
                    load_bias(pass_a)
                    load_qkv_a(ph, range(RAW, ph.units))
                elif ph.kind == "qkv":
                    if not peeled:
                        load_first(ph)
                    load_bias(pass_b[2 * ph.run.rnd + (ph.run.items[0][1] > 0)])
                    n0 = 4 * ph.run.rnd + 2 * (ph.run.items[0][1] > 0)
                    keep_small(1, n0, n0 + 2)
                    keep_small(0, n0, n0 + 2)
                    load_units(ph, 1)
                else:
                    if ph is down[0, 0]:
                        load_norms()
                        repeat_lines()
                    if ph.kind == "down" and ph.l == 0:
                        load_decode_constants(ph.f)
                    load_units(ph, peeled)
                peeled = int(ph.kind == "qkv")
                if peeled:
                    load_first(ph.next)
                if ph is qkv[0]:
                    load_decode(0)
                if ph is qkv[1, 1, 1]:
                    load_decode(1)
            for f in range(2 * DEPTH):
                sp.wait_ge(copy_done[f], 16 * RAW * (UP_ITS + DOWN_ITS))
            sp.wait_ge(copy_done[2 * DEPTH], 16 * 2 * 4)
            sp.wait_ge(new_done, 16 * 4)
            sp.wait_ge(v_out, count["v"])
            for b in range(2):
                sp.wait_ge(kt_out[b], count["kt"][b])
                sp.wait_ge(ss_out[b], count["ss"][b])
            sp.wait_ge(out_done, 32)

        @block.tensor
        def _(pe):
            def gemm(slot, chunks, hi, lo, s, start, stop, x_lo0=None):
                for k in range(chunks):
                    if x_lo0 is not None:
                        pe.wait_ge(x_lo, x_lo0 + k + 1)
                    for h in range(2):
                        a = acc(s, h)
                        pe.matmul(a, wl[slot][:, k, :], hi(k)[:, halves[h]], start=start and k == 0, stop=False)
                        pe.matmul(a, wh[slot][:, k, :], lo(k)[:, halves[h]], start=False, stop=False)
                        last = pe.matmul(a, wh[slot][:, k, :], hi(k)[:, halves[h]], start=False, stop=stop and k == chunks - 1)
                return last

            def x_hi_(k):
                return xh[:, k, :]

            def x_lo_(k):
                return xl[:, k, :]

            def unit(ph, it, j, x_lo0=None):
                pe.wait_ge(wl_rdy, it * RAW + (ph.u0 + j + 5))
                if ph.kind == "down":
                    s, first, last = (j // 2) % 2, j % 2 == 0, j % 2 == 1
                    pe.wait_ge(hl_rdy, FC * ph.ffn + (FU if first else FC) + 2)
                    if first:
                        pe.wait_ge(acc_free[s], it + (ph.t0 // 2 + 2))
                    mm = gemm(j % 2, FU, lambda k: hh[:, (j % 2) * FU + k, :], lambda k: hl[:, (j % 2) * FU + k, :], s, first, last)
                else:
                    pe.wait_ge(acc_free[j % 2], it * 2 + (ph.t0 // 2 + j // 2 + 2))
                    mm = gemm(j % 2, KC, x_hi_, x_lo_, j % 2, True, True, x_lo0)
                mm.then_inc(mm_done, 1)

            def all_read(ph):
                for s in range(2):
                    pe.wait_ge(acc_free[s], (ph.t0 + ph.tiles) // 2 + 2)

            def add_to_mean(ph, it, s, stop=False):
                pe.wait_ge(acc_free[s], it + (ph.t0 // 2 + 3))
                for h in range(2):
                    v = z[:, bass.ds(it * 2 + s, 1), halves[h]].rearrange("p o n -> p (o n)")
                    mm = pe.matmul(bank[4 + h][:, 0:HALF], ones[:], v, start=False, stop=stop)
                return mm

            def project(ph):
                for h in range(2):
                    pe.matmul(bank[4 + h][:, 0:HALF], zeros[:], ones[:, 0:1].to_broadcast([P, HALF]), start=True, stop=False)

                def body(it, late):
                    for j in range(RAW):
                        unit(ph, it, j)
                        if ph.kind == "down":
                            if j % 2 and (late or j == 3):
                                add_to_mean(ph, it + (-1 if j == 1 else 0), j // 2 ^ 1)
                        elif late or j >= 2:
                            add_to_mean(ph, it * 2 + (j // 2 - 1), j % 2)
                body(0, False)
                with pe.Fori(1, ph.units // RAW) as it:
                    body(it, True)

            def norm(n, ph):
                last = KC // 2 - 1
                if ph.kind == "wo":
                    add_to_mean(ph, last, 0)
                mm = add_to_mean(ph, last, 1, True)
                mm.then_inc(ln_mean, 2)
                for h in range(2):
                    pe.wait_ge(ln_sq, 2 * n + h + 1)
                    for c in range(KC):
                        mm = pe.matmul(bank[6 + h][:, 0:HALF], ones[:], sq[:, c, halves[h]], start=c == 0, stop=c == KC - 1)
                    mm.then_inc(ln_var, 1)

            def tokens_major(R, b):
                for c in range(NBLK):
                    pe.transpose(bank[4 + b][:, c * P:(c + 1) * P], R["st"][b][:, c * P:(c + 1) * P], ident[:])
                pe.transpose(bank[6 + b][0:SAMPLE, 0:P], R["st"][b][:, SEQ:TOK], ident[:]).then_inc(tr_done, 1)

            def qkv_run(ph, x_lo0):
                r = ph.run

                def turn(it, j):
                    pe.wait_ge(acc_free[(j - 1) % 2], it * 2 + ((ph.t0 + j - 1) // 2 + 3))
                    pe.wait_ge(tr_free[(j - 1) % 2], it * 2 + ((r.tr0 + j - 1) // 2 + 2))
                    tokens_major(r.R, (j - 1) % 2)
                for j in range(RAW):
                    unit(ph, 0, j, x_lo0 if j == 0 else None)
                    if j:
                        turn(0, j)
                with pe.Fori(1, ph.units // RAW) as it:
                    for j in range(RAW):
                        unit(ph, it, j)
                        turn(it, j)
                turn(ph.units // RAW, 0)

            def attention(ps, run):
                R = ps.R
                all_read(run.ph)
                pe.wait_ge(qk_cp, run.cp_total)
                for b in range(2):
                    pe.wait_ge(tr_free[b], (run.tr0 + run.n) // 2 + 2)

                def scores(i, blk):
                    b = blk % 2
                    pe.wait_ge(qs_rdy, i * 4 + (ps.u0 + blk + 1))
                    pe.wait_ge(sm_done, i * 4 + (ps.u0 + blk + 1))
                    for hd in range(2):
                        if ps.dilated:
                            for g in range(2):
                                rhs = R["k"][g][:, bass.ds(i, 1), blk * P:(blk + 1) * P].rearrange("p o n -> p (o n)")
                                c = hd * 256 + g * P
                                mm = pe.matmul(bank[b][:, c:c + P], R["qs"][b][:, 2 * g + hd, :], rhs, start=True, stop=True)
                        else:
                            c0 = first_col(ps, blk)
                            kt_ = i // 4 if ps is pass_a else i
                            rhs = R["k"][0][:, bass.ds(kt_, 1), (blk - 1) * P + c0:(blk + 1) * P].rearrange("p o n -> p (o n)")
                            mm = pe.matmul(bank[b][:, hd * 256 + c0:(hd + 1) * 256], R["qs"][b][:, hd, :], rhs, start=True, stop=True)
                    mm.then_inc(sc_done, 1)

                def turn(i, blk):
                    b = blk % 2
                    pe.wait_ge(ex_done, i * 4 + (ps.u0 + blk + 1))
                    pe.wait_ge(ptc_done, i * 4 + (ps.u0 + blk + 1))
                    for hd in range(2):
                        for kb in range(first_col(ps, blk) // P, 2):
                            c = hd * 256 + kb * P
                            mm = pe.transpose(bank[4 + b][:, c:c + P], R["st"][b][:, c:c + P], ident[:])
                    mm.then_inc(pt_done, 1)

                def values(i, blk):
                    b = blk % 2
                    pe.wait_ge(ptc_done, i * 4 + (ps.u0 + blk + 3))
                    pe.wait_ge(oev_done, i * 4 + (ps.u0 + blk + 1))
                    vt = i // 4 if ps is pass_a else i
                    for hd in range(2):
                        kbs = range(first_col(ps, blk) // P, 2)
                        for kb in kbs:
                            if ps.dilated:
                                src = R["v"][kb][:, blk, bass.ds(vt * P, P)]
                            else:
                                src = R["v"][0][:, blk - 1 + kb, bass.ds(vt * P, P)]
                            c = hd * 256 + kb * P
                            mm = pe.matmul(bank[2 + b][:, hd * P:(hd + 1) * P], R["kt"][b][:, c:c + P], src,
                                           start=kb == kbs[0], stop=kb == kbs[-1])
                    mm.then_inc(pv_done, 1)
                skewed(pe, ps.pairs, [(scores, 0), (turn, 1), (values, 2)])
                end = ps.u0 + ps.units
                pe.wait_ge(sm_done, end + 2)
                pe.wait_ge(ptc_done, end + 2)
                pe.wait_ge(oev_done, end + 2)

            def outputs_a():
                for b in range(NBLK):
                    pe.wait_ge(ow_rdy, b + 1)
                for p_ in range(PAIRS):
                    if p_ >= 2:
                        pe.wait_ge(ot_v, p_ - 1)
                    for b in range(NBLK):
                        mm = pe.transpose(bank[6 + p_ % 2][:, b * P:(b + 1) * P], RA["o"][0][:, b, p_ * P:(p_ + 1) * P], ident[:])
                    mm.then_inc(ot_done, 1)

            def outputs_b(r):
                pe.wait_ge(ow_rdy, NBLK + 8 * (r + 1))
                for p_ in range(4):
                    if p_:
                        pe.wait_ge(ot_v, PAIRS + 4 * r + p_)
                    for y in range(2):
                        for b in range(NBLK):
                            mm = pe.transpose(bank[6 + y][:, b * P:(b + 1) * P], RB["o"][y][:, b, p_ * P:(p_ + 1) * P], ident[:])
                    mm.then_inc(ot_done, 1)

            def decode(layer):
                L = LAYER[layer]
                D, G, kv = L["D"], L["G"], L["kv"]
                if layer == 0:
                    pe.wait_ge(ot_v, PAIRS)
                else:
                    pe.wait_ge(ot_v, PAIRS + 8)
                nb = (kv * HD) // 256 // 2 or 1
                w = kv * HD // nb

                def broadcast(y):
                    tok = y.n * DEC + y.tau
                    if y.n == 0 and y.tau == 0:
                        pe.wait_ge(d_q2l, layer + y.g + 1)
                    for c in range(2):
                        if y.k:
                            pe.wait_ge(d_qb, 2 * (y.k - 1) + c + 1)
                        pe.matmul(bank[c][:], pick[:, tok:tok + 1].to_broadcast([P, P]),
                                  D["q2"][:, y.g, c * 512:(c + 1) * 512], start=True, stop=True).then_inc(d_qp, 1)

                def scores_by_row(T):
                    k = 4 * layer + T
                    pe.wait_ge(d_red, L["k"][L["per"] * (T + 1) - 1].prods[-1].k + 1)
                    if T:
                        pe.wait_ge(d_sv, k)
                    for g in range(G):
                        mm = pe.transpose(bank[4][:, g * P:(g + 1) * P], D["s"][:, g, T * P:(T + 1) * P], ident[:])
                    mm.then_inc(d_st, 1)

                def probs_by_key(T):
                    k = 4 * layer + T
                    pe.wait_ge(d_nm, 3 * k + 3)
                    if T:
                        pe.wait_ge(d_ptc, k)
                    for g in range(G):
                        mm = pe.transpose(bank[5][:, g * P:(g + 1) * P], D["sm"][T % 2][:, g * P:(g + 1) * P], ident[:])
                    mm.then_inc(d_pt, 1)
                    pe.wait_ge(d_ptc, k + 1)

                def cached_values(x):
                    n, g, taus = x.what
                    if g == 0 and n >= 2:
                        pe.wait_ge(d_msk, NS * layer + n - 1)
                    pe.wait_ge(d_kv[x.slot], x.val)
                    for tau in taus:
                        for c in range(nb):
                            mm = pe.matmul(bank[2 + 4 * (n % 2) + c][32 * tau:32 * tau + HEADS, 0:w], D["p"][:, g, n * DEC + tau, :],
                                           D["kv"][x.slot][:, c * w:(c + 1) * w], start=g == 0, stop=g == G - 1,
                                           tile_position=(0, 32 * tau), skip_group_check=True)
                    mm.then_inc(d_pv, 1)
                for p_ in range(-1, L["end"]):
                    if part_at(L, p_, 2) is not None:
                        probs_by_key(part_at(L, p_, 2))
                    if part_at(L, p_, 0) is not None:
                        scores_by_row(part_at(L, p_, 0))
                    if keys_at(L, p_ + 1):
                        for y in keys_at(L, p_ + 1).prods:
                            broadcast(y)
                    if p_ < 0:
                        continue
                    if values_at(L, p_):
                        cached_values(values_at(L, p_))
                pe.wait_ge(d_sum, layer + 1)
                for p_ in range(PAIRS):
                    src = D["qn"][0:SAMPLE, 0, :] if layer == 0 else D["ot"][0:SAMPLE, :]
                    mm = pe.transpose(bank[4][:, p_ * SAMPLE:(p_ + 1) * SAMPLE], src[:, p_ * P:(p_ + 1) * P], ident[0:SAMPLE, 0:SAMPLE])
                mm.then_inc(d_tt, 1)
                pe.wait_ge(d_tv, layer + 1)

            pe.wait_ge(cst_ld, 16 * 5)
            pe.wait_ge(setup, 2)
            pe.matmul(bank[0][0:HEADS, :], tab[:], oh1[:, 0:512], start=True, stop=True)
            pe.matmul(bank[1][0:HEADS, 0:LINES - 512], tab[:], oh1[:, 512:LINES], start=True, stop=True)
            pe.matmul(bank[2][0:HEADS, 0:ND], tab[:], oh2[:], start=True, stop=True).then_inc(line_t, 1)
            pe.wait_ge(in_ld, 32)
            pe.wait_ge(line_c, 1)
            for c in range(KC):
                if c >= 4:
                    pe.wait_ge(ln_aff, c - 3)
                for b in range(NBLK):
                    pe.transpose(bank[c % 4][:, b * P:(b + 1) * P], xin[:, b, c * P:(c + 1) * P], ident[:])
                pe.transpose(bank[4 + c % 4][:, 0:SAMPLE], xsin[:, c * P:(c + 1) * P], ident[0:SAMPLE, 0:SAMPLE]).then_inc(init_t, 1)

            n_norm = 0
            for ph in phases:
                if ph.kind == "up":
                    for j in range(RAW):
                        unit(ph, 0, j, KC * n_norm if j == 0 else None)
                    with pe.Fori(1, ph.units // RAW) as it:
                        for j in range(RAW):
                            unit(ph, it, j)
                elif ph.kind == "down":
                    project(ph)
                    norm(n_norm, ph)
                    n_norm += 1
                elif ph.kind == "qkv":
                    qkv_run(ph, KC * n_norm)
                    if ph is qkv[0]:
                        attention(pass_a, ph.run)
                        outputs_a()
                        decode(0)
                    else:
                        r, y = ph.run.rnd, int(ph.run.items[0][1] > 0)
                        attention(pass_b[2 * r + y], ph.run)
                        if y:
                            outputs_b(r)
                            if r:
                                pe.wait_ge(sp_l, 2)
                                decode(1)
                            else:
                                pe.wait_ge(ot_v, PAIRS + 4)
                else:
                    project(ph)
                    norm(n_norm, ph)
                    n_norm += 1
            pe.wait_ge(ln_aff, KC * (3 * DEPTH + 1))
            for b in range(NBLK + 1):
                if b >= 2:
                    pe.wait_ge(out_ca, b - 1)
                    pe.wait_ge(out_cv, b - 1)
                w = P if b < NBLK else SAMPLE
                for c in range(KC):
                    mm = pe.transpose(bank[2 * (b % 2) + c // 4][0:w, (c % 4) * P:(c % 4 + 1) * P], z[:, c, b * P:b * P + w], ident[:])
                mm.then_inc(out_t, 1)

        def units_ahead(eng, ph, split, read):
            n = ph.units // RAW
            with eng.Fori(0, n - 1) as it:
                for j in range(RAW):
                    split(ph, it * RAW + (j + 1), (j + 1) % RAW, it + (j + 1) // RAW)
                    read(ph, it, j)
            for j in range(RAW):
                if j < RAW - 1:
                    split(ph, RAW * (n - 1) + j + 1, j + 1, n - 1)
                elif ph.next:
                    split(ph.next, 0, 0, 0)
                read(ph, n - 1, j)

        def stage_tile(eng, copy, r, i):
            st, s, g = r.R["st"][i % 2], i % 2, r.items[i][1]
            eng.wait_ge(mm_done, r.ph.u0 + i + 3)
            if r.tr0 + i > 1:
                eng.wait_ge(tr_done, r.tr0 + i - 1)
            if i >= 2 and r.items[i - 2][2] != "v":
                eng.wait_ge(qk_cp, r.cp_after[i - 2])
            if g == 0:
                copy(st[:, halves[0]], acc(s, 0))
                copy(st[:, halves[1]], acc(s, 1)).then_inc(acc_free[s], 1)
            else:
                u0, u1 = HALF // 4, (SEQ - HALF) // 4
                v = st[:, 0:SEQ].rearrange("p (c u) -> p c u", c=4)
                copy(v[:, :, 0:u0], acc(s, 0).rearrange("p (u c) -> p c u", c=4))
                copy(v[:, :, u0:u0 + u1], acc(s, 1)[:, 0:SEQ - HALF].rearrange("p (u c) -> p c u", c=4))
                copy(st[:, SEQ:TOK], acc(s, 1)[:, SEQ - HALF:HALF]).then_inc(acc_free[s], 1)

        def keep_tokens(eng, copy, r, i):
            b, (gi, g, kind, p_) = i % 2, r.items[i]
            eng.wait_ge(tr_done, r.tr0 + i + 1)
            if kind == "k":
                if r.kt_before[i]:
                    eng.wait_ge(kt_out[b], r.kt_before[i])
                copy(r.R["kt"][b][:], bank[4 + b][:])
            if kind == "v":
                if r.v_total > 16 * 4:
                    eng.wait_ge(v_out, r.v_before)
                copy(r.R["v"][gi][:, :, p_ * P:(p_ + 1) * P], bank[4 + b][:].rearrange("p (c n) -> p c n", c=NBLK))
            if r.ss_before[i]:
                eng.wait_ge(ss_out[b], r.ss_before[i])
            copy(r.R["ss"][b][:], bank[6 + b][0:SAMPLE, 0:P]).then_inc(tr_free[b], 1)
        for n_, r in enumerate(runs):
            r.v_before = runs[n_ - 1].v_total if n_ else 0

        @block.scalar
        def _(act):
            def split(ph, i, j, it):
                act.wait_ge(raw_in[j], it * (16 * ph.dmas) + (ph.land0[j] + 16 * ph.dmas))
                act.wait_ge(mm_done, i + (ph.u0 + 1))
                act.copy(wh[j % 2][:, 0:ph.chunks, :], raw[j][:, 0:ph.chunks, :]).then_inc(wh_rdy, 1)

            def read(ph, it, j):
                if ph.kind == "up" and j % 2 == 0:
                    b = j // 2
                    act.wait_ge(mm_done, it * RAW + (ph.u0 + j + 3))
                    act.wait_ge(acc_free[1], it * 2 + (ph.t0 // 2 + b + 1))
                    act.activation(sil[b][:, halves[0]], acc(0, 0), ACT.Silu)
                    act.activation(sil[b][:, halves[1]], acc(0, 1), ACT.Silu).then_inc(acc_free[0], 1)

            def norm(n, last):
                if n == 0:
                    act.wait_ge(norm_ld, 16 * 6 * DEPTH)
                for h in range(2):
                    act.wait_ge(ln_dev, 2 * n + h + 1)
                    act.activation(sq[:, :, halves[h]], z[:, :, halves[h]], ACT.Square).then_inc(ln_sq, 1)
                for h in range(2):
                    act.wait_ge(ln_rs, 2 * (2 * n + h) + 2)
                    act.activation(rstd[:, halves[h]], rstd[:, halves[h]], ACT.Sqrt).then_inc(ln_root, 1)
                for c in range(KC):
                    act.wait_ge(ln_nrm, KC * n + c + 1)
                    act.activation(z[:, c, :], z[:, c, :], ACT.Identity, bias=shift[:, n, c:c + 1]).then_inc(ln_aff, 1)
                    if not last:
                        high(n + 1, c)

            def high(k, c):
                act.wait_ge(ln_aff, KC * k + c + 1)
                act.copy(xh[:, c, :], z[:, c, :]).then_inc(x_hi, 1)

            def run(ph):
                r = ph.run
                for i in range(r.n):
                    if i + 1 < r.n:
                        split(ph, i + 1, (i + 1) % RAW, (i + 1) // RAW)
                    else:
                        split(ph.next, 0, 0, 0)
                    if i % 2 == 0:
                        stage_tile(act, act.copy, r, i)
                    if i >= 1 and (i - 1) % 2 == 1:
                        keep_tokens(act, act.copy, r, i - 1)
                keep_tokens(act, act.copy, r, r.n - 1)

            def attention(ps, rn):
                R = ps.R
                for b in range(2):
                    act.wait_ge(kt_out[b], rn.kt_total[b])

                def exps(i, blk):
                    b, c0 = blk % 2, first_col(ps, blk)
                    act.wait_ge(nm_done, i * 4 + (ps.u0 + blk + 1))
                    for hd in range(2):
                        x = R["st"][b][:, hd * 256 + c0:(hd + 1) * 256]
                        last = act.activation(x, x, ACT.Exp, bias=R["nm"][b][:, hd:hd + 1], accum_out=R["dn"][b][:, hd:hd + 1])
                    last.then_inc(ex_done, 1)

                def copy(i, blk):
                    b, c0 = blk % 2, first_col(ps, blk)
                    act.wait_ge(pt_done, i * 4 + (ps.u0 + blk + 3))
                    act.wait_ge(pv_done, i * 4 + (ps.u0 + blk + 1))
                    v = R["kt"][b][:].rearrange("p (h k) -> p h k", h=2)[:, :, c0:256]
                    act.copy(v, bank[4 + b][:].rearrange("p (h k) -> p h k", h=2)[:, :, c0:256]).then_inc(ptc_done, 1)
                skewed(act, ps.pairs, [(exps, 0), (copy, 1)])

            def weights(k):
                R, y = (RA, 0) if k == 0 else (RB, (k - 1) % 2)
                act.wait_ge(cmb_v, 7 * k + 3)
                act.activation(R["t"][1][:], R["t"][1][:], ACT.Exp)
                act.activation(R["t"][2][:], R["t"][2][:], ACT.Exp).then_inc(cmb_a, 1)

            def outputs_a():
                for p_ in range(PAIRS):
                    act.wait_ge(ot_done, p_ + 1)
                    act.copy(xh[:, p_, 0:SEQ], bank[6 + p_ % 2][:]).then_inc(ot_a, 1)

            def keep_high(r):
                act.wait_ge(ot_v, PAIRS + 4 * (r + 1))
                act.copy(xh[:, 4 * r:4 * r + 4, 0:SEQ], RB["at"][:]).then_inc(sp_h, 1)

            def outputs_b(r):
                if r:
                    keep_high(0)
                    act.wait_ge(sp_l, 1)
                for p_ in range(4):
                    act.wait_ge(ot_done, PAIRS + 4 * r + p_ + 1)
                    if p_ >= 2:
                        act.wait_ge(ot_v, PAIRS + 4 * r + p_ - 1)
                    act.copy(RB["st"][p_ % 2][:, 0:SEQ], bank[6][:]).then_inc(ot_a, 1)
                if r:
                    keep_high(1)

            def decode(layer):
                L = LAYER[layer]
                D, G, kv, new = L["D"], L["G"], L["kv"], L["new"]
                act.wait_ge(d_qn, 32 * (layer + 1))
                act.wait_ge(d_zero, 2 * layer + 1)
                for g in range(G):
                    act.copy(D["q2"][0:2 * SAMPLE, g], D["qn"][:, g]).then_inc(d_q2, 1)
                W = G * P + new + (1 if layer == 0 else 0)
                n0 = sum(len(x.prods) for x in L["k"][0:L["per"]])

                def copy_query(y):
                    m = y.k - L["prod"][0].k
                    if m >= 3:
                        act.wait_ge(*L["prod"][m - 3].mult)
                    for c in range(2):
                        act.wait_ge(d_qp, 2 * y.k + c + 1)
                        act.copy(D["qb"][y.slot][:, c * 512:(c + 1) * 512], bank[c][:]).then_inc(d_qb, 1)
                    if m == n0 * 5 // 8:
                        act.wait_ge(d_nv, L["kn"][-1].done[0][1])
                        act.dma_start(snew_d[layer].rearrange("(s h) c -> s (h c)", h=HEADS), D["snew"][:].rearrange("s h c -> s (h c)")).then_inc(d_sn_out, 16)
                    if m == n0 - 1:
                        act.wait_ge(d_sn_out, 16 * (layer + 1))
                        act.dma_start(D["snb"][:], snew_d[layer].rearrange("(t p) c -> p t c", p=P)).then_inc(d_sn_in, 16)
                for p_ in range(L["end"]):
                    if keys_at(L, p_):
                        for y in keys_at(L, p_).prods:
                            copy_query(y)
                    if part_at(L, p_, 2) is not None:
                        cached_probs(layer, part_at(L, p_, 2))
                    if part_at(L, p_, 2) == 3:
                        act.wait_ge(d_nm, 3 * (4 * layer + 3) + 3)
                        act.dma_start(pnew_d[layer].rearrange("(t p) c -> p t c", p=P), D["pnb"][:]).then_inc(d_pn_out, 16)
                        act.wait_ge(d_pn_out, 16 * (layer + 1))
                        act.dma_start(D["pn"][:].rearrange("s h c -> s (h c)"), pnew_d[layer].rearrange("(s h) c -> s (h c)", h=HEADS)).then_inc(d_pn_in, 16)
                    T = part_at(L, p_, 0)
                    if T is not None:
                        k, sm = 4 * layer + T, D["sm"][T % 2]
                        act.wait_ge(d_nm, 3 * k + 1)
                        act.activation(sm[:, 0:W], sm[:, 0:W], ACT.Exp, bias=D["st"][:, T, 0:1], accum_out=D["st"][:, T, 1:2]).then_inc(d_ex, 1)
                act.wait_ge(d_oc, NS * (layer + 1))
                for tau in range(DEC):
                    dst = odec_d[layer].rearrange("(n t) (h d) -> t h n d", t=DEC, d=HD)[tau]
                    act.dma_start(dst, D["oc"][32 * tau:32 * tau + HEADS, :, :]).then_inc(d_oc_out, 16)
                act.wait_ge(d_oc_out, 16 * DEC * (layer + 1))
                act.dma_start(D["ot"][0:SAMPLE, :], odec_d[layer]).then_inc(d_ot_in, 16)
                act.wait_ge(d_tt, layer + 1)
                act.copy(xh[:, :, SEQ:TOK], bank[4][:, 0:KC * SAMPLE].rearrange("p (c s) -> p c s", c=KC)).then_inc(d_ta, 1)

            def cached_probs(layer, T):
                D, G = LAYER[layer]["D"], LAYER[layer]["G"]
                act.wait_ge(d_pt, 4 * layer + T + 1)
                for g in range(G):
                    v = bank[5][:, g * P:(g + 1) * P].rearrange("p (s h) -> p s h", h=HEADS)
                    last = act.copy(D["p"][:, g, 8 * T:8 * T + 8, 0:HEADS], v)
                last.then_inc(d_ptc, 1)

            act.wait_ge(cst_ld, 16 * 5)
            act.copy(pick[:], pick32[:])
            act.wait_ge(line_c, 2)
            act.dma_start(once_d, lin1[:]).then_inc(line_o, 16)
            act.dma_start(dec_lines_d, lin2[:]).then_inc(line_o, 16)
            for c in range(KC):
                act.wait_ge(init_t, c + 1)
                act.copy(z[:, c, 0:SEQ], bank[c % 4][:])
                act.copy(z[:, c, SEQ:TOK], bank[4 + c % 4][:, 0:SAMPLE]).then_inc(ln_aff, 1)
                high(0, c)
            split(phases[0], 0, 0, 0)
            act.wait_ge(line_o, 32)
            n_norm = 0
            for ph in phases:
                if ph.kind == "qkv":
                    run(ph)
                    if ph is qkv[0]:
                        attention(pass_a, ph.run)
                        weights(0)
                        outputs_a()
                        decode(0)
                    else:
                        r, y = ph.run.rnd, int(ph.run.items[0][1] > 0)
                        attention(pass_b[2 * r + y], ph.run)
                        if y:
                            weights(1 + 2 * r)
                            weights(2 + 2 * r)
                            outputs_b(r)
                            if r:
                                decode(1)
                else:
                    units_ahead(act, ph, split, read)
                    if ph.kind != "up":
                        norm(n_norm, ph.next is None)
                        n_norm += 1
            for b in range(NBLK + 1):
                w = P if b < NBLK else SAMPLE
                act.wait_ge(out_t, b + 1)
                act.copy(yout[0:w, b, 0:512], bank[2 * (b % 2)][0:w, :]).then_inc(out_ca, 1)
            act.wait_ge(out_ca, NBLK + 1)
            act.wait_ge(out_cv, NBLK + 1)
            act.dma_start(o["y_prompt"][0].rearrange("(b p) d -> p b d", p=P), yout[:, 0:NBLK, :]).then_inc(out_done, 16)
            act.dma_start(o["y_sample"].rearrange("n t d -> (n t) d"), yout[0:SAMPLE, NBLK, :]).then_inc(out_done, 16)

        @block.vector
        def _(dve):
            steps = {"cmb": 0}

            def split(ph, i, j, it):
                dve.wait_ge(wh_rdy, i + (ph.u0 + 1))
                v = wh[j % 2][:, 0:ph.chunks, :]
                dve.tensor_tensor(wl[j % 2][:, 0:ph.chunks, :], raw[j][:, 0:ph.chunks, :], v.bitcast(F32), ALU.subtract).then_inc(wl_rdy, 1)

            def read(ph, it, j):
                if ph.kind == "up" and j % 2 == 1:
                    b = j // 2
                    dve.wait_ge(mm_done, it * RAW + (ph.u0 + j + 3))
                    dve.wait_ge(acc_free[0], it * 2 + (ph.t0 // 2 + b + 3))
                    dve.wait_ge(hl_rdy, it * 2 + (FC * ph.ffn + b + 1))
                    for h in range(2):
                        last = dve.tensor_tensor(h32[b][:, halves[h]], sil[b][:, halves[h]], acc(1, h), ALU.mult)
                    last.then_inc(acc_free[1], 1)
                elif ph.kind == "down" and j % 2 == 1:
                    add_tile(ph, it * RAW + (ph.u0 + j + 3), it * 2 + j // 2, j // 2, 0.5)
                elif ph.kind == "wo":
                    add_tile(ph, it * RAW + (ph.u0 + j + 3), it * RAW + j, j % 2, 1.0)

            def add_tile(ph, done, chunk, s, factor):
                dve.wait_ge(mm_done, done)
                for h in range(2):
                    v = z[:, bass.ds(chunk, 1), halves[h]].rearrange("p o n -> p (o n)")
                    last = dve.scalar_tensor_tensor(v, acc(s, h), factor, v, ALU.mult, ALU.add)
                last.then_inc(acc_free[s], 1)

            def norm(n, last):
                if n == 0:
                    dve.wait_ge(norm_ld, 16 * 6 * DEPTH)
                for h in range(2):
                    v = z[:, :, halves[h]]
                    dve.wait_ge(ln_mean, 2 * n + h + 1)
                    m = bank[4 + h][:, None, 0:HALF].to_broadcast([P, KC, HALF])
                    dve.tensor_tensor(v, v, m, ALU.subtract).then_inc(ln_dev, 1)
                for h in range(2):
                    dve.wait_ge(ln_var, 2 * n + h + 1)
                    dve.tensor_scalar(rstd[:, halves[h]], bank[6 + h][:, 0:HALF], LN_EPS, None, ALU.add).then_inc(ln_rs, 1)
                    dve.wait_ge(ln_rs, 2 * (2 * n + h) + 1)
                    dve.reciprocal(rstd[:, halves[h]], rstd[:, halves[h]]).then_inc(ln_rs, 1)
                dve.wait_ge(ln_root, 2 * n + 2)
                for c in range(KC):
                    dve.scalar_tensor_tensor(z[:, c, :], z[:, c, :], gain[:, n, c:c + 1], rstd[:], ALU.mult, ALU.mult).then_inc(ln_nrm, 1)
                    if not last and c >= 2:
                        low(n + 1, c - 2)
                if not last:
                    for c in range(KC - 2, KC):
                        low(n + 1, c)

            def low(k, c):
                dve.wait_ge(x_hi, KC * k + c + 1)
                dve.tensor_tensor(xl[:, c, :], z[:, c, :], xh[:, c, :].bitcast(F32), ALU.subtract).then_inc(x_lo, 1)

            def run(ph):
                r = ph.run
                for i in range(r.n):
                    if i + 1 < r.n:
                        split(ph, i + 1, (i + 1) % RAW, (i + 1) // RAW)
                    else:
                        split(ph.next, 0, 0, 0)
                    if i % 2 == 1:
                        stage_tile(dve, dve.tensor_copy, r, i)
                    if i >= 1 and (i - 1) % 2 == 0:
                        keep_tokens(dve, dve.tensor_copy, r, i - 1)

            def attention(ps, rn):
                R = ps.R
                dve.wait_ge(bias_ld, BIAS_LD[ps.n])

                def add_bias(i, blk):
                    b, c0 = blk % 2, first_col(ps, blk)
                    dve.wait_ge(sc_done, i * 4 + (ps.u0 + blk + 3))
                    dve.wait_ge(pt_done, i * 4 + (ps.u0 + blk + 1))
                    x = R["st"][b][:, 0:SEQ].rearrange("p (h k) -> p h k", h=2)[:, :, c0:256]
                    s = bank[b][:].rearrange("p (h k) -> p h k", h=2)[:, :, c0:256]
                    dve.scalar_tensor_tensor(x, s, SCALE, R["bias"][:, bass.ds(i * 2, 2), c0:256], ALU.mult, ALU.add).then_inc(sm_done, 1)
                    dve.wait_ge(sm_done, i * 4 + (ps.u0 + blk + 3))
                    dve.tensor_reduce(R["nm"][b][:], x, AX_X, ALU.max, negate=True).then_inc(nm_done, 1)

                def output(i, blk):
                    b = blk % 2
                    dve.wait_ge(pv_done, i * 4 + (ps.u0 + blk + 3))
                    o_ = R["o"][ps.slot][:, blk, bass.ds(i * P, P)].rearrange("p (h d) -> p h d", h=2)
                    dve.tensor_copy(o_, bank[2 + b][:, 0:256].rearrange("p (a d) -> p a d", d=HD)[:, 0:4:3, :]).then_inc(oev_done, 1)

                def stats(i, blk):
                    b = blk % 2
                    dve.wait_ge(ex_done, i * 4 + (ps.u0 + blk + 1))
                    md = R["md"][ps.slot]
                    dve.tensor_copy(md[:, blk, 0, bass.ds(i * 2, 2)], R["nm"][b][:])
                    dve.tensor_copy(md[:, blk, 1, bass.ds(i * 2, 2)], R["dn"][b][:]).then_inc(st_done, 1)
                skewed(dve, ps.pairs, [(add_bias, 0), (stats, 1), (output, 3)])

            def step(ins):
                steps["cmb"] += 1
                ins.then_inc(cmb_v, 1)
                dve.wait_ge(cmb_v, steps["cmb"])

            def weights(k):
                R, y = (RA, 0) if k == 0 else (RB, (k - 1) % 2)
                own, oth, tt = R["md"][y], R["mo"][y], R["t"]
                if k:
                    dve.wait_ge(md_in, 16 * (2 * ((k - 1) // 2) + 2))
                step(dve.tensor_tensor(tt[0][:], own[:, :, 0, :], oth[:, :, 0, :], ALU.min))
                step(dve.tensor_tensor(tt[1][:], tt[0][:], own[:, :, 0, :], ALU.subtract))
                step(dve.tensor_tensor(tt[2][:], tt[0][:], oth[:, :, 0, :], ALU.subtract))
                dve.wait_ge(cmb_a, k + 1)
                step(dve.tensor_tensor(tt[3][:], tt[1][:], own[:, :, 1, :], ALU.mult))
                step(dve.tensor_tensor(tt[4][:], tt[2][:], oth[:, :, 1, :], ALU.mult))
                step(dve.tensor_tensor(tt[3][:], tt[3][:], tt[4][:], ALU.add))
                dve.reciprocal(tt[3][:], tt[3][:]).then_inc(cmb_r, 1)
                dve.wait_ge(cmb_r, k + 1)
                step(dve.tensor_tensor(tt[1][:], tt[1][:], tt[3][:], ALU.mult))
                n = HEADS if k == 0 else PAIRS
                for b in range(NBLK):
                    v = R["o"][y][:, b, :].rearrange("p (h d) -> p h d", d=HD)
                    dve.tensor_tensor(v, v, tt[1][:, b, :, None].to_broadcast([P, n, HD]), ALU.mult).then_inc(ow_rdy, 1)

            def outputs_a():
                for p_ in range(PAIRS):
                    dve.wait_ge(ot_a, p_ + 1)
                    dve.tensor_tensor(xl[:, p_, 0:SEQ], bank[6 + p_ % 2][:], xh[:, p_, 0:SEQ].bitcast(F32), ALU.subtract).then_inc(ot_v, 1)

            def keep_low(r):
                dve.wait_ge(sp_h, r + 1)
                dve.tensor_tensor(xl[:, 4 * r:4 * r + 4, 0:SEQ], RB["at"][:], xh[:, 4 * r:4 * r + 4, 0:SEQ].bitcast(F32), ALU.subtract).then_inc(sp_l, 1)

            def outputs_b(r):
                if r:
                    keep_low(0)
                    dve.wait_ge(sp_l, 1)
                for p_ in range(4):
                    dve.wait_ge(ot_a, PAIRS + 4 * r + p_ + 1)
                    v = RB["at"][:, p_, :].rearrange("p (u c) -> p u c", c=4)
                    y = bank[7][:].rearrange("p (c u) -> p u c", c=4)
                    x = RB["st"][p_ % 2][:, 0:SEQ].rearrange("p (u c) -> p u c", c=4)
                    dve.tensor_tensor(v, y, x, ALU.add).then_inc(ot_v, 1)
                if r:
                    keep_low(1)

            def decode(layer):
                L = LAYER[layer]
                D, G, kv, new = L["D"], L["G"], L["kv"], L["new"]
                rep = HEADS // kv
                low_rows = slice(SAMPLE, 2 * SAMPLE)
                for g in range(G):
                    dve.wait_ge(d_q2, layer + g + 1)
                    dve.tensor_tensor(D["q2"][low_rows, g], D["qn"][low_rows, g], D["q2"][low_rows, g].bitcast(F32), ALU.subtract).then_inc(d_q2l, 1)
                nv = [L["nv0"]]

                def nstep(ins):
                    nv[0] += 1
                    ins.then_inc(d_nv, 1)

                def heads_of(ap):
                    v = ap.rearrange("p (k d) -> p k d", d=HD)
                    return v[:, :, None, :].to_broadcast([ap.shape[0], kv, rep, HD])

                def by_head(ap):
                    return ap.rearrange("p (k r d) -> p k r d", r=rep, d=HD)

                def new_key(x):
                    c_, g, tp = x.what
                    dve.wait_ge(d_kn[x.slot], x.landed)
                    nstep(dve.tensor_tensor(by_head(D["ot"][0:SAMPLE, :]), heads_of(D["kn"][x.slot][:]), by_head(D["qn"][0:SAMPLE, g, :]), ALU.mult))
                    dve.wait_ge(d_nv, nv[0])
                    nstep(dve.tensor_reduce(D["snew"][:, :, c_:c_ + 1].rearrange("s h c -> s (h c)"), D["ot"][0:SAMPLE, :].rearrange("s (h d) -> s h d", d=HD), AX_X, ALU.add))
                    dve.wait_ge(d_nv, nv[0])

                def product(y):
                    dve.wait_ge(d_kv[y.tile.slot], y.tile.val)
                    dve.wait_ge(d_qb, 2 * y.k + 2)
                    if y.k >= 3:
                        dve.wait_ge(d_red, y.k - 2)
                    dve.tensor_tensor(by_head(D["pr"][y.slot][:]), heads_of(D["kv"][y.tile.slot][:]), by_head(D["qb"][y.slot][:]), ALU.mult).then_inc(d_mult[1], 1)

                W = G * P + new + (1 if layer == 0 else 0)

                def shift_max(T):
                    k, sm = 4 * layer + T, D["sm"][T % 2]
                    dve.wait_ge(d_st, k + 1)
                    if T >= 2:
                        dve.wait_ge(d_pt, k - 1)
                    dve.scalar_tensor_tensor(sm[:, 0:G * P], bank[4][:, 0:G * P], SCALE, D["bc"][:].rearrange("p g r -> p (g r)"),
                                             ALU.mult, ALU.add).then_inc(d_sv, 1)
                    dve.scalar_tensor_tensor(sm[:, G * P:G * P + new], D["snb"][:, T, :], SCALE, D["bn"][:], ALU.mult, ALU.add).then_inc(d_sx, 1)
                    if layer == 0:
                        dve.tensor_copy(sm[:, W - 1:W], D["snk"][:]).then_inc(d_sx, 1)
                        dve.wait_ge(d_sx, 2 * k + 2)
                    else:
                        dve.wait_ge(d_sx, 8 + T + 1)
                    dve.wait_ge(d_sv, k + 1)
                    dve.tensor_reduce(D["st"][:, T, 0:1], sm[:, 0:W], AX_X, ALU.max, negate=True).then_inc(d_nm, 1)

                def normalise(T):
                    k, sm = 4 * layer + T, D["sm"][T % 2]
                    dve.wait_ge(d_ex, k + 1)
                    dve.reciprocal(D["st"][:, T, 2:3], D["st"][:, T, 1:2]).then_inc(d_nm, 1)
                    dve.wait_ge(d_nm, 3 * k + 2)
                    dve.tensor_scalar(D["pnb"][:, T, :], sm[:, G * P:G * P + new], D["st"][:, T, 2:3], None, ALU.mult)
                    dve.tensor_scalar(sm[:, 0:G * P], sm[:, 0:G * P], D["st"][:, T, 2:3], None, ALU.mult).then_inc(d_nm, 1)
                nb = (kv * HD) // 256 // 2 or 1

                def own_heads(n, end):
                    dve.wait_ge(d_pv, end)
                    if n:
                        dve.wait_ge(d_oc, NS * layer + n)
                    w = kv * HD // nb
                    tmp = D["ot"]
                    for c in range(nb):
                        q = w // HD
                        m = D["mask"][:, c * q:(c + 1) * q, None].to_broadcast([P, q, HD])
                        src = bank[2 + 4 * (n % 2) + c][:, 0:w].rearrange("p (h d) -> p h d", d=HD)
                        last = dve.tensor_tensor(tmp[:, c * w:(c + 1) * w].rearrange("p (h d) -> p h d", d=HD), src, m, ALU.mult)
                    last.then_inc(d_msk, 1)
                    dve.wait_ge(d_msk, NS * layer + n + 1)
                    dve.tensor_reduce(D["oc"][:, n, :], tmp[:, 0:kv * HD].rearrange("p (h d) -> p d h", d=HD), AX_X, ALU.add).then_inc(d_oc, 1)

                added, term = D["pr"][0][0:SAMPLE, :], D["pr"][1][0:SAMPLE, :]

                def new_value(i, x):
                    c_, g, tp = x.what
                    if i == 0:
                        dve.wait_ge(d_pn_in, 16 * (layer + 1))
                        dve.wait_ge(d_red, L["prod"][-1].k + 1)
                        nv[0] = x.done[0][1] - 2
                    dve.wait_ge(d_kn[x.slot], x.landed)
                    p_ = D["pn"][:, :, c_:c_ + 1].rearrange("s (k r) c -> s k r c", r=rep).to_broadcast([SAMPLE, kv, rep, HD])
                    out = term if i else added
                    nstep(dve.tensor_tensor(by_head(out), heads_of(D["kn"][x.slot][:]), p_, ALU.mult))
                    dve.wait_ge(d_nv, nv[0])
                    if i:
                        nstep(dve.tensor_tensor(added, added, term, ALU.add))
                        dve.wait_ge(d_nv, nv[0])
                    else:
                        dve.sem_inc(d_nv, 1)
                        nv[0] += 1

                news = list(L["kn"])
                due = None
                for p_ in range(L["end"]):
                    if keys_at(L, p_):
                        for y in keys_at(L, p_).prods:
                            if y.by:
                                product(y)
                            dve.wait_ge(*y.mult)
                            tok = y.n * DEC + y.tau
                            dve.tensor_reduce(D["s"][:, y.g, tok * HEADS:(tok + 1) * HEADS], D["pr"][y.slot][:].rearrange("p (h d) -> p h d", d=HD),
                                              AX_X, ALU.add).then_inc(d_red, 1)
                            if news:
                                new_key(news.pop(0))
                    if part_at(L, p_, 1) is not None:
                        normalise(part_at(L, p_, 1))
                    T = part_at(L, p_, 0)
                    if T is not None:
                        if T == 0:
                            dve.wait_ge(d_cst, 16 * (cst_dmas[0] + (cst_dmas[1] if layer else 0)))
                            dve.wait_ge(d_sn_in, 16 * (layer + 1))
                        shift_max(T)
                    if due:
                        own_heads(*due)
                        due = None
                    for i, x in enumerate(L["vn"]):
                        if p_ == new_value_at(L, i):
                            new_value(i, x)
                    x = values_at(L, p_)
                    if x and x.what[1] == G - 1 and x.what[2][-1] == DEC - 1:
                        due = (x.what[0], x.done[0][1])
                own_heads(*due)
                dve.wait_ge(d_ot_in, 16 * (layer + 1))
                dve.tensor_tensor(D["ot"][0:SAMPLE, :], D["ot"][0:SAMPLE, :], added, ALU.add).then_inc(d_add, 1)
                dve.wait_ge(d_add, layer + 1)
                tmp = D["qn"][0:SAMPLE, 0, :]
                if layer == 0:
                    dst = tmp.rearrange("s (g r h d) -> s g h r d", g=2, h=2, d=HD)
                    src = D["ot"][0:SAMPLE, :].rearrange("s (g h r d) -> s g h r d", g=2, h=2, d=HD)
                    for g in range(2):
                        last = dve.tensor_copy(dst[:, g], src[:, g])
                    last.then_inc(d_sum, 1)
                else:
                    dve.sem_inc(d_sum, 1)
                dve.wait_ge(d_ta, layer + 1)
                v = bank[4][:, 0:KC * SAMPLE].rearrange("p (c s) -> p c s", c=KC)
                dve.tensor_tensor(xl[:, :, SEQ:TOK], v, xh[:, :, SEQ:TOK].bitcast(F32), ALU.subtract).then_inc(d_tv, 1)

            dve.memset(tab[NUM_BUCKETS:NUM_BUCKETS + 1, :], 1.0).then_inc(setup, 1)
            dve.wait_ge(line_t, 1)
            dve.tensor_copy(lin1[:, 0:512], bank[0][0:HEADS, :])
            dve.tensor_copy(lin1[:, 512:LINES], bank[1][0:HEADS, 0:LINES - 512])
            dve.tensor_copy(lin2[:], bank[2][0:HEADS, 0:ND]).then_inc(line_c, 2)
            for c in range(KC):
                low(0, c)
            split(phases[0], 0, 0, 0)
            dve.wait_ge(line_o, 32)
            n_norm = 0
            for ph in phases:
                if ph.kind == "qkv":
                    run(ph)
                    if ph is qkv[0]:
                        attention(pass_a, ph.run)
                        mo = RA["mo"][0]
                        for b in range(NBLK):
                            dve.tensor_scalar(mo[:, b, 0, :], RA["sink"][:], -1.0, None, ALU.mult)
                        dve.memset(mo[:, :, 1, :], 1.0).then_inc(sink_rdy, 1)
                        dve.wait_ge(sink_rdy, 1)
                        dve.wait_ge(st_done, pass_a.units)
                        dve.wait_ge(oev_done, pass_a.units + 2)
                        weights(0)
                        outputs_a()
                        decode(0)
                    else:
                        r, y = ph.run.rnd, int(ph.run.items[0][1] > 0)
                        attention(pass_b[2 * r + y], ph.run)
                        if y:
                            ps = pass_b[2 * r + 1]
                            dve.wait_ge(st_done, ps.u0 + ps.units)
                            dve.wait_ge(oev_done, ps.u0 + ps.units + 2)
                            weights(1 + 2 * r)
                            weights(2 + 2 * r)
                            outputs_b(r)
                            if r:
                                decode(1)
                else:
                    if ph.kind != "up":
                        dve.wait_ge(ln_ax, KC * (n_norm + 1))
                    units_ahead(dve, ph, split, read)
                    if ph.kind != "up":
                        norm(n_norm, ph.next is None)
                        n_norm += 1
            for b in range(NBLK + 1):
                w = P if b < NBLK else SAMPLE
                dve.wait_ge(out_t, b + 1)
                dve.tensor_copy(yout[0:w, b, 512:1024], bank[2 * (b % 2) + 1][0:w, :]).then_inc(out_cv, 1)

        @block.gpsimd
        def _(pool):
            def scale_x(k):
                for c in range(KC):
                    pool.wait_ge(x_lo, KC * k + c + 1)
                    pool.tensor_scalar(z[:, c, :], z[:, c, :], ALPHA, None, ALU.mult).then_inc(ln_ax, 1)

            def hidden(ph):
                with pool.Fori(0, FC // 2) as it:
                    for b in range(2):
                        pool.wait_ge(acc_free[1], it * 2 + (ph.t0 // 2 + b + 3))
                        hi = hh[:, bass.ds(it * 2 + b, 1), :].rearrange("p o n -> p (o n)")
                        lo = hl[:, bass.ds(it * 2 + b, 1), :].rearrange("p o n -> p (o n)")
                        pool.tensor_copy(hi, h32[b][:]).then_inc(hh_rdy, 1)
                        pool.wait_ge(hh_rdy, it * 2 + (FC * ph.ffn + b + 1))
                        pool.tensor_tensor(lo, h32[b][:], hi.bitcast(F32), ALU.subtract).then_inc(hl_rdy, 1)

            def store_out(r, i):
                b, (gi, g, kind, p_) = i % 2, r.items[i]
                layer = r.layer
                pool.wait_ge(tr_free[b], (r.tr0 + i) // 2 + 3)
                col = (4 * r.rnd + p_) * P
                ss = r.R["ss"][b][:]
                if kind == "q" and layer == 0:
                    dst = q_d[0][:, 0, :].rearrange("s (g h r d) -> s g h r d", g=2, h=2, d=HD)[:, p_ // 4, :, p_ % 4, :]
                    pool.dma_start(dst, ss.rearrange("s (h d) -> s h d", h=2)).then_inc(ss_out[b], 16)
                elif kind == "q":
                    pool.dma_start(q_d[1][:, g, col:col + P], ss).then_inc(ss_out[b], 16)
                else:
                    pool.dma_start(kv_d[layer][:, g, int(kind == "v"), col:col + P], ss).then_inc(ss_out[b], 16)
                if kind == "q":
                    return
                w = int(kind == "v")
                dst = states_p[layer, g][0, 0].rearrange("r w h d -> r w (h d)")[:, w, col:col + P]
                if kind == "k":
                    src, s_ = r.R["kt"][b][:].rearrange("p (c n) -> p c n", c=NBLK), kt_out[b]
                else:
                    src, s_ = r.R["v"][gi][:, :, p_ * P:(p_ + 1) * P], v_out
                if g == 0:
                    pool.dma_start(dst, src[:, NBLK - 1, :]).then_inc(s_, 16)
                else:
                    pool.dma_start(dst.rearrange("(u c) n -> u c n", c=NBLK), src).then_inc(s_, 16)

            def run(ph):
                r = ph.run
                if ph is not qkv[0] and ph is not qkv[1, 0, 0]:
                    k = runs.index(r)
                    prev = PASS_OF[k - 1]
                    pool.wait_ge(sc_done, prev.u0 + prev.units + 2)
                for i, (gi, g, kind, p_) in enumerate(r.items):
                    if kind != "v":
                        pool.wait_ge(acc_free[i % 2], (ph.t0 + i) // 2 + 3)
                        pool.tensor_copy(r.R[kind][gi][:, p_, :], r.R["st"][i % 2][:, 0:SEQ]).then_inc(qk_cp, 1)
                    if i:
                        store_out(r, i - 1)
                store_out(r, r.n - 1)

            def clear_staging(layer):
                R = RB if layer else RA
                pool.wait_ge(ln_var, 2 * (norm_index(layer, 0) + 1))
                for b in range(2):
                    last = pool.memset(R["qs"][b][:], 0.0)
                last.then_inc(qs_zero, 1)
                pool.wait_ge(qs_zero, layer + 1)

            def attention(ps, rn):
                R = ps.R
                pool.wait_ge(qk_cp, rn.cp_total)

                def stage(i, blk):
                    b = blk % 2
                    pool.wait_ge(sc_done, i * 4 + (ps.u0 + blk + 1))
                    for g in range(2 if ps.dilated else 1):
                        for hd in range(2):
                            rows = slice(hd * HD, (hd + 1) * HD)
                            src = R["q"][g][rows, bass.ds(i, 1), blk * P:(blk + 1) * P].rearrange("p o n -> p (o n)")
                            last = pool.tensor_copy(R["qs"][b][rows, 2 * g + hd, :], src)
                    last.then_inc(qs_rdy, 1)
                skewed(pool, ps.pairs, [(stage, 0)])

            def exchange(ps):
                r = (ps.n - 1) // 2
                pool.wait_ge(st_done, ps.u0 + ps.units)
                pat = "(u c) e -> u c e" if ps.dilated else "(c u) e -> u c e"
                pool.dma_start(md_d[r, ps.slot].rearrange(pat, c=NBLK), RB["md"][ps.slot][:].rearrange("p b k h -> p b (k h)")).then_inc(md_out, 16)

            def fetch(r):
                pool.wait_ge(md_out, 32 * (r + 1))
                for y in range(2):
                    pat = "(u c) e -> u c e" if y else "(c u) e -> u c e"
                    pool.dma_start(RB["mo"][y][:].rearrange("p b k h -> p b (k h)"), md_d[r, 1 - y].rearrange(pat, c=NBLK)).then_inc(md_in, 16)

            def decode(layer):
                L = LAYER[layer]
                D, kv = L["D"], L["kv"]
                rep = HEADS // kv
                r = L["runs"][-1]
                if layer == 0:
                    pool.wait_ge(ot_v, PAIRS)
                else:
                    pool.wait_ge(sp_l, 2)
                pool.wait_ge(v_out, r.v_total)
                for b in range(2):
                    pool.wait_ge(kt_out[b], r.kt_total[b])
                    pool.wait_ge(ss_out[b], r.ss_total[b])
                pool.memset(D["q2"][:].bitcast(F32), 0.0).then_inc(d_zero, 1)
                pool.memset(D["p"][:], 0.0).then_inc(d_zero, 1)
                for y in L["prod"]:
                    if y.by:
                        continue
                    pool.wait_ge(d_kv[y.tile.slot], y.tile.val)
                    pool.wait_ge(d_qb, 2 * y.k + 2)
                    if y.k >= 3:
                        pool.wait_ge(d_red, y.k - 2)
                    kk = D["kv"][y.tile.slot][:].rearrange("p (k d) -> p k d", d=HD)[:, :, None, :].to_broadcast([P, kv, rep, HD])
                    pool.tensor_tensor(D["pr"][y.slot][:].rearrange("p (k r d) -> p k r d", r=rep, d=HD), kk,
                                       D["qb"][y.slot][:].rearrange("p (k r d) -> p k r d", r=rep, d=HD), ALU.mult).then_inc(d_mult[0], 1)
                for g in range(L["G"]):
                    c = states_s[layer, g]
                    R_ = c.shape[2]
                    dst = c[0][:, R_ - DEC:R_].rearrange("n t w h d -> n t (w h d)")
                    src = kv_d[layer][:, g].rearrange("(n t) w f -> n t (w f)", t=DEC)
                    pool.dma_start(dst, src).then_inc(new_done, 16)

            for s_, n_ in ((mm_done, 2), (acc_free[0], 2), (acc_free[1], 2), (wl_rdy, 4), (hl_rdy, 2), (tr_free[0], 2),
                           (tr_free[1], 2), (sc_done, 2), (sm_done, 2), (pt_done, 2), (ptc_done, 2), (pv_done, 2), (oev_done, 2)):
                pool.sem_inc(s_, n_)
            pool.memset(zeros[:], 0.0)
            pool.memset(ones[:], 1.0 / D_MODEL).then_inc(setup, 1)
            scale_x(0)
            pool.wait_ge(line_o, 32)
            n_norm = 0
            for ph in phases:
                if ph.kind == "up":
                    hidden(ph)
                elif ph.kind in ("down", "wo"):
                    n_norm += 1
                    if ph.kind == "down" and ph.f == 0:
                        clear_staging(ph.l)
                    if ph.next:
                        scale_x(n_norm)
                else:
                    run(ph)
                    if ph is qkv[0]:
                        attention(pass_a, ph.run)
                        decode(0)
                    else:
                        r, y = ph.run.rnd, int(ph.run.items[0][1] > 0)
                        attention(pass_b[2 * r + y], ph.run)
                        exchange(pass_b[2 * r + y])
                        if y:
                            fetch(r)
                            if r:
                                decode(1)


_INS = ["x_prompt", "x_sample", "cache_a_kv", "cache_b1_kv", "cache_b2_kv", "cache_b3_kv", "rel_bias_table", "ln_gain",
        "ln_bias", "ffn_w_gate", "ffn_w_up", "ffn_w_down", "attn_a_w_qkv", "attn_a_w_o", "attn_a_sinks", "attn_b_w_qkv",
        "attn_b_w_o"]
_OUTS = [("y_prompt", (1, 512, 1024)), ("y_sample", (8, 4, 1024)), ("state_a_p", (1, 1, 128, 2, 4, 64)),
         ("state_b1_p", (1, 1, 128, 2, 16, 64)), ("state_b2_p", (1, 1, 512, 2, 16, 64)), ("state_b3_p", (1, 1, 512, 2, 16, 64)),
         ("state_a_s", (1, 8, 128, 2, 4, 64)), ("state_b1_s", (1, 8, 128, 2, 16, 64)), ("state_b2_s", (1, 8, 512, 2, 16, 64)),
         ("state_b3_s", (1, 8, 2048, 2, 16, 64))]


def constants():
    p = np.arange(P)[:, None] % 32
    return {"c_ident": np.eye(P, dtype=np.float32), "c_lines": one_hot_lines(), "c_dec": one_hot_decode(),
            "c_pick": ((np.arange(P)[:, None] % SAMPLE == np.arange(SAMPLE)[None]) & (np.arange(P)[:, None] < 2 * SAMPLE)).astype(np.float32),
            "c_mask_a": (p // 4 == np.arange(KV_A)[None]).astype(np.float32) * (p < HEADS),
            "c_mask_b": (p == np.arange(HEADS)[None]).astype(np.float32)}


def kernel(**inputs):
    import concourse.bacc as bacc
    from concourse.bass_utils import run_bass_kernel_spmd

    nc = bacc.Bacc("TRN2", target_bir_lowering=False, num_devices=1)
    arrays, t, o = {}, {}, {}
    for name, a in {**{n: inputs[n] for n in _INS}, **constants()}.items():
        a = np.ascontiguousarray(a)
        if name.startswith("c_"):
            a = a.astype(np.float32)
        arrays[f"in_{name}"] = a
        t[name] = nc.dram_tensor(f"in_{name}", a.shape, mybir.dt.from_np(a.dtype), kind="ExternalInput").ap()
    for name, shape in _OUTS:
        o[name] = nc.dram_tensor(f"out_{name}", shape, F32, kind="ExternalOutput").ap()
    build(nc, t, o)
    r = run_bass_kernel_spmd(nc, [arrays], core_ids=[0])
    return tuple(r.results[0][f"out_{name}"] for name, _ in _OUTS)
```
